# Optimizing a Trainium2 kernel written in Bass

```python
import jax, jax.numpy as jnp
from jax import lax
import numpy as np

D_MODEL = 1024
BATCH = 1
SEQ = 1024
DEPTH = 1

CHUNK = 64
D_MIX = D_MODEL
DN_HEADS = 4
DN_HEAD_DIM = 128
DN_WIDTH = DN_HEADS * DN_HEAD_DIM
SHORT_CONV = 4
POOL_WIDTH = D_MIX - DN_WIDTH
POOL_WINDOWS = (2, 4, 8, 16)
POOL_GROUPS = len(POOL_WINDOWS)
POOL_GROUP_DIM = POOL_WIDTH // POOL_GROUPS
D_FF = ((8 * D_MODEL // 3) + 127) // 128 * 128
FFN_CONV = 3
EPS = 1e-6
IN_COLS = 4 * DN_WIDTH + 2 * DN_HEADS + POOL_WIDTH

kernel_name = 'hybrid_deltanet_multipool_convffn'

def rmsnorm(x, w):
    xf = x.astype(jnp.float32)
    y = xf * lax.rsqrt(jnp.mean(xf * xf, axis=-1, keepdims=True) + EPS)
    return (y * w.astype(jnp.float32)).astype(x.dtype)

def l2norm(x):
    return x * lax.rsqrt(jnp.sum(x * x, axis=-1, keepdims=True) + EPS)

def causal_dwconv(x, w):
    k_width = w.shape[0]
    t_len = x.shape[1]
    xp = jnp.pad(x, ((0, 0), (k_width - 1, 0), (0, 0)))
    y = xp[:, 0:t_len] * w[0]
    for i in range(1, k_width):
        y = y + xp[:, i:i + t_len] * w[i]
    return y

def chunk_gated_delta_rule(q, k, v, g, beta):
    bsz, t_len, n_h, d_k = q.shape
    d_v = v.shape[-1]
    n_c = t_len // CHUNK

    def to_chunks(t):
        t = t.reshape((bsz, n_c, CHUNK, n_h) + t.shape[3:])
        return jnp.moveaxis(t, 3, 1)

    q, k, v, g, beta = (to_chunks(t) for t in (q, k, v, g, beta))
    G = jnp.cumsum(g, axis=-1)
    idx = jnp.arange(CHUNK)
    incl = idx[:, None] >= idx[None, :]
    strict = idx[:, None] > idx[None, :]
    diff = G[..., :, None] - G[..., None, :]
    gamma = jnp.exp(jnp.where(incl, diff, -jnp.inf))
    kk = jnp.einsum('bhnid,bhnjd->bhnij', k, k)
    a_mat = jnp.where(strict, kk * beta[..., :, None] * gamma, 0.0) + jnp.eye(CHUNK, dtype=q.dtype)
    eg = jnp.exp(G)
    rhs = jnp.concatenate([v * beta[..., None], k * (beta * eg)[..., None]], axis=-1)
    sol = lax.linalg.triangular_solve(a_mat, rhs, left_side=True, lower=True, unit_diagonal=True)
    u, w = sol[..., :d_v], sol[..., d_v:]
    qg = q * eg[..., None]
    aqk = jnp.einsum('bhnid,bhnjd->bhnij', q, k) * gamma
    kd = k * jnp.exp(G[..., -1:] - G)[..., None]
    glast = jnp.exp(G[..., -1])
    xs = tuple(jnp.moveaxis(t, 2, 0) for t in (u, w, qg, aqk, kd, glast))

    def step(S, inp):
        u_c, w_c, qg_c, aqk_c, kd_c, gl_c = inp
        v_new = u_c - jnp.einsum('bhck,bhkv->bhcv', w_c, S)
        o_c = jnp.einsum('bhck,bhkv->bhcv', qg_c, S) + jnp.einsum('bhij,bhjv->bhiv', aqk_c, v_new)
        S = S * gl_c[..., None, None] + jnp.einsum('bhck,bhcv->bhkv', kd_c, v_new)
        return S, o_c

    S0 = jnp.zeros((bsz, n_h, d_k, d_v), jnp.float32)
    _, o = lax.scan(step, S0, xs)
    return o.transpose(1, 0, 3, 2, 4).reshape(bsz, t_len, n_h, d_v)

def gated_deltanet(qkv_raw, z, b_raw, a_raw, conv_w, a_log, dt_bias, onorm_w):
    bsz, t_len, _ = qkv_raw.shape
    qkv = jax.nn.silu(causal_dwconv(qkv_raw, conv_w)).astype(jnp.float32)
    q, k, v = jnp.split(qkv, 3, axis=-1)
    heads = lambda t: t.reshape(bsz, t_len, DN_HEADS, DN_HEAD_DIM)
    q = l2norm(heads(q)) * (DN_HEAD_DIM ** -0.5)
    k = l2norm(heads(k))
    v = heads(v)
    beta = jax.nn.sigmoid(b_raw.astype(jnp.float32))
    g = -jnp.exp(a_log.astype(jnp.float32)) * jax.nn.softplus(
        a_raw.astype(jnp.float32) + dt_bias.astype(jnp.float32))
    o = chunk_gated_delta_rule(q, k, v, g, beta)
    o = rmsnorm(o, onorm_w) * jax.nn.silu(heads(z).astype(jnp.float32))
    return o.reshape(bsz, t_len, DN_WIDTH).astype(qkv_raw.dtype)

def multiscale_pool(u, pool_w, pool_b, pool_scale):
    bsz, t_len, _ = u.shape
    ug = u.astype(jnp.float32).reshape(bsz, t_len, POOL_GROUPS, POOL_GROUP_DIM)
    cs = jnp.cumsum(ug, axis=1)
    pos = jnp.arange(1, t_len + 1, dtype=jnp.float32)
    pooled = []
    for gi, win in enumerate(POOL_WINDOWS):
        c = cs[:, :, gi]
        lagged = jnp.pad(c, ((0, 0), (win, 0), (0, 0)))[:, :t_len]
        cnt = jnp.minimum(pos, float(win))[None, :, None]
        pooled.append((c - lagged) / cnt)
    d = jnp.stack(pooled, axis=2) - ug
    y = jnp.einsum('btgc,gcd->btgd', d, pool_w.astype(jnp.float32)) + pool_b.astype(jnp.float32)
    return (y.reshape(bsz, t_len, POOL_WIDTH) * pool_scale.astype(jnp.float32)).astype(u.dtype)

def setup_inputs(seed: int = 0) -> dict:
    key = jax.random.key(seed)
    ks = jax.random.split(key, 20)
    f32 = jnp.float32
    nrm = lambda k, shape, scale: jax.random.normal(k, shape, f32) * scale
    x = jax.random.normal(ks[0], (BATCH, SEQ, D_MODEL), f32)
    norm1_w = 1.0 + nrm(ks[1], (DEPTH, D_MODEL), 0.02)
    w_in = nrm(ks[2], (DEPTH, D_MODEL, IN_COLS), D_MODEL ** -0.5)
    conv_qkv_w = nrm(ks[3], (DEPTH, SHORT_CONV, 3 * DN_WIDTH), SHORT_CONV ** -0.5)
    a_log = jnp.log(jax.random.uniform(ks[4], (DEPTH, DN_HEADS), f32, 1.0, 16.0))
    dt = jnp.exp(jax.random.uniform(ks[5], (DEPTH, DN_HEADS), f32, math_log(1e-3), math_log(0.1)))
    dt_bias = dt + jnp.log(-jnp.expm1(-dt))
    onorm_w = 1.0 + nrm(ks[6], (DEPTH, DN_HEAD_DIM), 0.02)
    pool_w = nrm(ks[7], (DEPTH, POOL_GROUPS, POOL_GROUP_DIM, POOL_GROUP_DIM), POOL_GROUP_DIM ** -0.5)
    pool_b = nrm(ks[8], (DEPTH, POOL_GROUPS, POOL_GROUP_DIM), 0.01)
    pool_scale = 1.0 + nrm(ks[9], (DEPTH, POOL_WIDTH), 0.02)
    w_out = nrm(ks[10], (DEPTH, D_MIX, D_MODEL), D_MIX ** -0.5)
    norm2_w = 1.0 + nrm(ks[11], (DEPTH, D_MODEL), 0.02)
    w_up = nrm(ks[12], (DEPTH, D_MODEL, 2 * D_FF), D_MODEL ** -0.5)
    ffn_conv_w = nrm(ks[13], (DEPTH, FFN_CONV, 2 * D_FF), FFN_CONV ** -0.5)
    ffn_conv_b = nrm(ks[14], (DEPTH, 2 * D_FF), 0.01)
    w_down = nrm(ks[15], (DEPTH, D_FF, D_MODEL), D_FF ** -0.5)
    final_norm_w = 1.0 + nrm(ks[16], (D_MODEL,), 0.02)
    return {'x': x, 'norm1_w': norm1_w, 'w_in': w_in, 'conv_qkv_w': conv_qkv_w,
            'a_log': a_log, 'dt_bias': dt_bias, 'onorm_w': onorm_w, 'pool_w': pool_w,
            'pool_b': pool_b, 'pool_scale': pool_scale, 'w_out': w_out, 'norm2_w': norm2_w,
            'w_up': w_up, 'ffn_conv_w': ffn_conv_w, 'ffn_conv_b': ffn_conv_b,
            'w_down': w_down, 'final_norm_w': final_norm_w}

def math_log(v):
    return float(np.log(v))

def reference(x, norm1_w, w_in, conv_qkv_w, a_log, dt_bias, onorm_w, pool_w, pool_b,
              pool_scale, w_out, norm2_w, w_up, ffn_conv_w, ffn_conv_b, w_down, final_norm_w):
    c_q = 3 * DN_WIDTH
    c_z = 4 * DN_WIDTH
    c_b = c_z + DN_HEADS
    c_a = c_b + DN_HEADS
    for l in range(DEPTH):
        h = rmsnorm(x, norm1_w[l])
        proj = h @ w_in[l]
        o_a = gated_deltanet(proj[..., :c_q], proj[..., c_q:c_z], proj[..., c_z:c_b],
                             proj[..., c_b:c_a], conv_qkv_w[l], a_log[l], dt_bias[l], onorm_w[l])
        o_b = multiscale_pool(proj[..., c_a:], pool_w[l], pool_b[l], pool_scale[l])
        x = x + jnp.concatenate([o_a, o_b], axis=-1) @ w_out[l]
        h = rmsnorm(x, norm2_w[l])
        up = causal_dwconv(h @ w_up[l], ffn_conv_w[l]) + ffn_conv_b[l]
        gate, val = jnp.split(up, 2, axis=-1)
        x = x + (jax.nn.silu(gate) * val) @ w_down[l]
    return rmsnorm(x, final_norm_w)


_drawn_inputs = setup_inputs


def setup_inputs(seed=0):
    import zlib

    import numpy as np

    out = dict(_drawn_inputs(seed))
    spreads = {}
    factors = {'norm1_w': 3.208,
     'onorm_w': 22.995,
     'pool_b': 8.0,
     'pool_scale': 18.905,
     'norm2_w': 13.2,
     'ffn_conv_b': 27.12,
     'final_norm_w': 8.161}
    for name, (base, spread) in spreads.items():
        noise = np.random.default_rng([zlib.crc32(name.encode()), seed]).standard_normal(out[name].shape)
        drawn = base * np.exp(spread * noise) if base else spread * noise
        out[name] = __import__('jax').numpy.asarray(drawn.astype(out[name].dtype))
    for name, factor in factors.items():
        out[name] = (out[name] * factor).astype(out[name].dtype)
    return out
```

```python
from contextlib import ExitStack

import concourse.bass as bass
import numpy as np
from concourse import mybir

F32 = mybir.dt.float32
F32R = mybir.dt.float32r
I32 = mybir.dt.int32
ALU = mybir.AluOpType
ACT = mybir.ActivationFunctionType

P = 128
BANK = 512
CHUNK = 64
HEADS = 4
EPS = 1e-6
POOL_WINDOWS = (2, 4, 8, 16)
LN_EXP_SET = "natural_log_exp_and_others"
LEVELS = 5

STEPS = ([("start", 3), ("sumsq_q", 3), ("sumsq_k", 6), ("decay", 3), ("norm_o", 5), ("decay_row", 3),
          ("vT", 4), ("beta_kk", 5), ("qk", 5), ("kT", 5)]
         + [s for lv in range(LEVELS) for s in ((f"level{lv}a", 5), (f"level{lv}b", 3))]
         + [("u", 4), ("w", 4)]
         + [s for c in range(16) for s in ((f"chunk{c}a", 3), (f"chunk{c}b", 3))])


def block_program(nc, x, norm1_w, w_in, conv_qkv_w, a_log, dt_bias, onorm_w, pool_w, pool_b,
                  pool_scale, w_out, norm2_w, w_up, ffn_conv_w, ffn_conv_b, w_down, final_norm_w, out):
    SEQ, D = x.shape[1], x.shape[2]
    KT = D // P
    TT = SEQ // P
    HALF = SEQ // 2
    DN = HEADS * P
    PG = len(POOL_WINDOWS)
    FT = w_down.shape[1] // P
    FG = FT // 2
    NCH = SEQ // CHUNK
    assert HALF == BANK and TT == 8 and FT % 2 == 0 and FG % 2 == 1

    x_t = x[0].rearrange("(t p) d -> t p d", p=P)
    out_t = out[0].rearrange("(t p) d -> t p d", p=P)
    w_in_k = w_in[0].rearrange("(k p) n -> p k n", p=P)
    w_up_k = w_up[0].rearrange("(k p) n -> p k n", p=P)
    w_out_k = w_out[0].rearrange("(k p) n -> k p n", p=P)
    w_down_k = w_down[0].rearrange("(f p) n -> f p n", p=P)

    def in_proj_column(i, j):
        return j * DN + i * P if i < HEADS else 4 * DN + 2 * HEADS + (PG - 1 - j) * P

    with ExitStack() as ctx:
        def sb(name, shape, dt=F32):
            return ctx.enter_context(nc.sbuf_tensor(name, shape, dt))

        def sem(name):
            return ctx.enter_context(nc.semaphore(name))

        a_hi = sb("a_hi", [P, KT, SEQ], F32R)
        with nc.sbuf_tensor("a_lo", [P, KT, SEQ], F32R) as a_lo:
            pass
        mlp = sb("mlp", [P, 8 * SEQ])
        act_hi, act_lo = a_hi[:, 0:4, :], a_hi[:, 4:8, :]
        up_raw = mlp[:, 0:4 * SEQ].rearrange("p (e g t) -> p e g t", e=2, g=2)
        up_conv = mlp[:, 4 * SEQ:8 * SEQ].rearrange("p (e g t) -> p e g t", e=2, g=2)

        B_WORDS = 18432
        with ExitStack() as early:
            early.enter_context(nc.sbuf_tensor("early_gap", [P, 6 * SEQ], F32))
            rows = early.enter_context(nc.sbuf_tensor("rows", [P, 11, P], F32))
            col_i = early.enter_context(nc.sbuf_tensor("col_i", [P, CHUNK], I32))
            row_i = early.enter_context(nc.sbuf_tensor("row_i", [P, CHUNK], I32))
            xor_i = early.enter_context(nc.sbuf_tensor("xor_i", [P, CHUNK], I32))
            shift_i = early.enter_context(nc.sbuf_tensor("shift_i", [P, 6, CHUNK], I32))
            wba = early.enter_context(nc.sbuf_tensor("wba", [P, KT, 8], F32))
            wba_hi = early.enter_context(nc.sbuf_tensor("wba_hi", [P, KT, 8], F32R))
            wba_lo = early.enter_context(nc.sbuf_tensor("wba_lo", [P, KT, 8], F32R))
            ba_T = early.enter_context(nc.sbuf_tensor("ba_T", [8, SEQ], F32))
            ba = early.enter_context(nc.sbuf_tensor("ba", [P, 8, TT], F32))
            sc = early.enter_context(nc.sbuf_tensor("sc", [P, 6, HEADS, TT], F32))
        with ExitStack() as late:
            h2_hi = late.enter_context(nc.sbuf_tensor("h2_hi", [P, KT, SEQ], F32R))
            h2_lo = late.enter_context(nc.sbuf_tensor("h2_lo", [P, KT, SEQ], F32R))
            with nc.sbuf_tensor("normed", [P, 2, D], F32) as normed:
                pass
            ring2_hi = late.enter_context(nc.sbuf_tensor("ring2_hi", [P, D], F32R))
            ring2_lo = late.enter_context(nc.sbuf_tensor("ring2_lo", [P, D], F32R))
        dn_all = sb("dn_all", [P, B_WORDS])
        used = [0]

        def dn(words):
            used[0] += words
            assert used[0] <= B_WORDS
            return dn_all[:, used[0] - words:used[0]]

        raw = dn(3 * SEQ).rearrange("p (j t) -> p j t", j=3)
        qkv = dn(3 * SEQ).rearrange("p (j t) -> p j t", j=3)
        qg = dn(SEQ)
        wT = dn(SEQ)
        v_tok = dn(SEQ)
        xinv = dn(TT * CHUNK)
        xinvT = dn(TT * CHUNK)
        t1 = dn(TT * CHUNK)
        r1 = dn(TT * CHUNK)
        r3 = dn(TT * CHUNK)
        r2 = dn(TT * CHUNK)
        gam = dn(2 * TT * CHUNK).rearrange("p (a n) -> p a n", a=2)
        gti = dn(TT * CHUNK)
        aqkT = dn(TT * CHUNK)
        tmp = dn(TT * CHUNK)
        state = dn(P)
        v_new = dn(P)
        k_be = dn(SEQ)
        k_d = dn(SEQ)
        o_T = dn(SEQ)
        bt = [r1, r3]
        ltT = r2
        res = sb("res", [P, TT, D])
        cat = res[:, :, :].rearrange("p t (k n) -> p t k n", n=P)
        stage = sb("stage", [P, 2, D])
        ring_hi01 = sb("ring_hi01", [P, 2, D], F32R)
        ring_lo01 = sb("ring_lo01", [P, 2, D], F32R)
        ring_hi = [ring_hi01[:, 0, :], ring_hi01[:, 1, :], ring2_hi[:, :]]
        ring_lo = [ring_lo01[:, 0, :], ring_lo01[:, 1, :], ring2_lo[:, :]]
        norm_row = sb("norm_row", [P, D])
        ident = sb("ident", [P, P])
        ones = sb("ones", [P, P])
        tri = sb("tri", [P, P])
        suf = sb("suf", [P, P])
        blk_ones = sb("blk_ones", [P, P])
        half_ones = sb("half_ones", [P, 2, P])
        m_le = sb("m_le", [P, CHUNK])
        m_gt = sb("m_gt", [P, CHUNK])
        m_lt = sb("m_lt", [P, CHUNK])
        m_eq = sb("m_eq", [P, CHUNK])
        m_pair = sb("m_pair", [P, CHUNK])
        m_level = sb("m_level", [P, 6, CHUNK])
        cols = sb("cols", [P, 11, 44])
        pool_wt = sb("pool_wt", [P, PG, P])
        pool_bias = sb("pool_bias", [P, PG])
        inv_pos = sb("inv_pos", [P, 16])
        decay_par = sb("decay_par", [P, 3, HEADS])
        beta = sb("beta", [P, HEADS, TT])
        g_tok = sb("g_tok", [P, HEADS, TT])
        beg = sb("beg", [P, HEADS, TT])
        ex = sb("ex", [P, 4, HEADS, TT])
        stats = sb("stats", [P, 3, TT])
        bias_q = sb("bias_q", [P, 1])
        eps_b = sb("eps_b", [P, 1])

        ps = ctx.enter_context(nc.psum_tensor("ps", [P, 8 * BANK], F32))

        def bank(b, n=1):
            return ps[:, b * BANK:(b + n) * BANK]

        x_in = [sem(f"x_in{t}") for t in range(TT)]
        stage_in = [sem(f"stage_in{s}") for s in range(2)]
        names = """rows_in ba_w_in par_in pool_w_in norm_row_in out_written
            iota_done cmp_done mask_done consts_done eps_done ident_done cols_T cols_done
            sq_done ln_done rstd_done normed_done normed_T h_hi h_lo ba_w_split ba_mm ba_evac ba_T_mm ba_done
            sc_act sc_dve cum_mm ex_done
            slab_hi slab_lo dense_done dense_evac
            conv_step silu_done pooled_step
            rhs_done sumsq_in sumsq_q_mm sumsq_k_mm v_T_mm vb_done lnq lnk rq rk qn_done kn_done
            decay_mm gam_done decay_row_mm erow_done gti_done g1_done beta_mm kk_mm qk_mm
            gtb_done lt_done l1_done x_upd xt_upd tmpt_done aqk_done qg_done k_T_mm kbe_done kd_done
            bt_done t1_mm t1_evac x_mm xt_mm u_mm u_evac w_mm w_evac
            v_mm v_new_done s_mm s_upd o_mm o_evac sqo_done sumsq_o_mm ln_o r_o on_done head_done
            wo_hi wo_lo ot_hi ot_lo res_mm res_add
            ffn_hi ffn_lo up_mm raw_evac up_conv_step gate_silu act_done act_hi_done act_lo_done
            final_sq final_ln final_r final_done""".split()
        S = {n: sem(n) for n in names}

        block = ctx.enter_context(nc.Block())

        def bc(scalars, n):
            return scalars.unsqueeze(2).to_broadcast([P, scalars.shape[1], n])

        def bm(mask, n=TT):
            return mask.unsqueeze(1).to_broadcast([P, n, CHUNK])

        def b3(ap, n=CHUNK):
            return ap.rearrange("p (b n) -> p b n", n=n)

        def o_bank(c):
            return (7, 5)[c // 8]

        def rows_of(par):
            return slice(CHUNK * par, CHUNK * par + CHUNK)

        GROUPS = [("proj", 0, j, h) for js in ((0, 1),) for h in range(2) for j in js]
        GROUPS += [("proj", i, j, h) for i in range(HEADS) for j in range(4) for h in range(2)
                   if i or j >= 2]
        pool = [[(kind, HEADS, j, h) for h in range(2)] for kind, j in
                (("proj", 0), ("proj", 1), ("lin", 0), ("proj", 2), ("lin", 1), ("proj", 3),
                 ("lin", 2), ("lin", 3))]
        GROUPS += [g for pair in pool for g in pair]
        INDEX = {g: n for n, g in enumerate(GROUPS)}
        NG = len(GROUPS)
        UNITS = [24 if g[0] == "proj" else 1 for g in GROUPS]
        PASS_START = [8 * i for i in range(HEADS + 1)]

        def groups_done(i, step):
            left, n = sum(f for _, f in STEPS[:step]), PASS_START[i]
            while n < NG and UNITS[n] <= left:
                left -= UNITS[n]
                n += 1
            return n

        def slab_used(n):
            return INDEX[("proj", n // 4, n % 4, 1)] + 1

        N_IN = 4 * (HEADS + 1)

        def load_up(sp, g, e, gu):
            first = gu * FT * P + e * P
            src = w_up_k[:, :, bass.ds(g * (2 * P) + first, P)]
            sp.dma_start(stage[:, gu, :].rearrange("p (k n) -> p k n", n=P), src)\
              .then_inc(stage_in[gu], 16)

        def load_down(sp, f, slot):
            src = w_down[0, bass.ds(f * P, P), :]
            sp.dma_start(stage[:, slot, :], src).then_inc(stage_in[slot], 16)

        @block.sync
        def _(sp):
            def slab(n):
                if n >= 2:
                    sp.wait_ge(S["slab_lo"], n - 1)
                c = in_proj_column(n // 4, n % 4)
                sp.dma_start(stage[:, n % 2, :].rearrange("p (k n) -> p k n", n=P),
                             w_in_k[:, :, c:c + P]).then_inc(stage_in[n % 2], 16)

            for t in range(TT):
                sp.dma_start(res[:, t, :], x_t[t]).then_inc(x_in[t], 16)
                if t in (3, 4):
                    slab(t - 3)
            sp.dma_start(decay_par[:, 0, :], a_log.to_broadcast([P, HEADS])).then_inc(S["par_in"], 16)
            sp.dma_start(decay_par[:, 1, :], dt_bias.to_broadcast([P, HEADS])).then_inc(S["par_in"], 16)
            sp.wait_ge(S["iota_done"], 1)
            sp.dma_start(rows[0:2 * FT, 0:3, :], ffn_conv_w[0].rearrange("a (r n) -> r a n", n=P))\
              .then_inc(S["rows_in"], 16)
            sp.dma_start(rows[0:2 * FT, 3, :], ffn_conv_b.rearrange("a (r n) -> (a r) n", n=P))\
              .then_inc(S["rows_in"], 16)
            sp.dma_start(rows[0:3 * HEADS, 4:8, :], conv_qkv_w[0].rearrange("a (r n) -> r a n", n=P))\
              .then_inc(S["rows_in"], 16)
            sp.dma_start(rows[0:PG, 8, :], pool_b[0]).then_inc(S["rows_in"], 16)
            sp.dma_start(rows[0:PG, 9, :], pool_scale.rearrange("a (r n) -> (a r) n", n=P))\
              .then_inc(S["rows_in"], 16)
            sp.dma_start(rows[0:1, 10, :], onorm_w).then_inc(S["rows_in"], 16)
            sp.dma_start(pool_wt[:, :, :], pool_w[0].rearrange("g c d -> c g d"))\
              .then_inc(S["pool_w_in"], 16)
            sp.wait_ge(S["normed_done"], TT)
            sp.dma_start(norm_row[:, :], norm2_w.to_broadcast([P, D])).then_inc(S["norm_row_in"], 16)
            for n in range(2, N_IN):
                slab(n)
            for k in range(KT):
                if k < 2:
                    sp.wait_ge(S["slab_lo"], N_IN - 1 + k)
                else:
                    sp.wait_ge(S["wo_lo"], k - 1)
                sp.dma_start(stage[:, k % 2, :], w_out_k[k]).then_inc(stage_in[k % 2], 16)
            for t in range(TT):
                sp.wait_ge(S["ot_lo"], t + 1)
                sp.dma_start(res[:, t, :], x_t[t]).then_inc(x_in[t], 16)
                if t == 0:
                    sp.wait_ge(S["wo_lo"], KT)
                    load_up(sp, 0, 0, 0)
                    load_up(sp, 0, 0, 1)
            sp.wait_ge(S["normed_done"], 2 * TT)
            sp.dma_start(norm_row[:, :], final_norm_w.unsqueeze(0).to_broadcast([P, D]))\
              .then_inc(S["norm_row_in"], 16)
            sp.wait_ge(S["ffn_lo"], 1)
            load_up(sp, 0, 1, 0)
            sp.wait_ge(S["ffn_lo"], 2)
            load_up(sp, 0, 1, 1)
            with sp.Fori(0, (FG - 1) // 2) as m:
                for b in range(2):
                    for n in range(6):
                        sp.wait_ge(S["ffn_lo"], m * 12 + (6 * b + n + 3))
                        if n < 4:
                            load_up(sp, m * 2 + (1 + b), n // 2, n % 2)
                        else:
                            load_down(sp, m * 4 + (2 * b + n - 4), n % 2)
            for e in range(2):
                sp.wait_ge(S["ffn_lo"], 4 + 6 * (FG - 1) + e - 1)
                load_down(sp, FT - 2 + e, e)
            for t in range(TT):
                sp.wait_ge(S["final_done"], t + 1)
                sp.dma_start(out_t[t], res[:, t, :]).then_inc(S["out_written"], 16)
            sp.wait_ge(S["out_written"], 16 * TT)

        STAGED = 16 * (N_IN + KT) // 2

        @block.gpsimd
        def _(pool_):
            pool_.memset(rows[:, :, :], 0.0).then_inc(S["iota_done"], 1)
            pool_.iota(col_i[:, :], pattern=[[1, CHUNK]], base=0, channel_multiplier=0)\
                .then_inc(S["iota_done"], 1)
            for par in range(2):
                pool_.wait_ge(S["iota_done"], 2 + par)
                pool_.iota(row_i[rows_of(par), :], pattern=[[0, CHUNK]], base=0,
                           channel_multiplier=1).then_inc(S["iota_done"], 1)
            pool_.wait_ge(S["iota_done"], 4)
            pool_.memset(ident[:, :], 0.0).then_inc(S["ident_done"], 1)
            pool_.wait_ge(S["ident_done"], 1)
            pool_.affine_select(out=ident[:, :], in_=ident[:, :], compare_op=ALU.not_equal, fill=1.0,
                                base=0, pattern=[[-1, P]], channel_multiplier=1)\
                .then_inc(S["ident_done"], 1)

            def slab_lo(n):
                pool_.wait_ge(S["slab_hi"], n + 1)
                pool_.tensor_tensor(ring_lo[n % 2], stage[:, n % 2, :], ring_hi[n % 2].bitcast(F32),
                                    ALU.subtract).then_inc(S["slab_lo"], 1)

            def right_sides(h):
                pool_.wait_ge(S["ex_done"], 1)
                if h:
                    pool_.wait_ge(S["xt_upd"], 6 * h)
                pool_.tensor_tensor(b3(r1), bc(g_tok[:, h, :], CHUNK), bm(m_gt[:, :]), ALU.mult)\
                    .then_inc(S["rhs_done"], 1)
                pool_.tensor_tensor(b3(r2), bc(g_tok[:, h, :], CHUNK), bm(m_le[:, :]), ALU.mult)\
                    .then_inc(S["rhs_done"], 1)
                pool_.tensor_tensor(b3(r3), bc(beta[:, h, :], CHUNK), bm(m_eq[:, :]), ALU.mult)\
                    .then_inc(S["rhs_done"], 1)

            for n in range(4):
                slab_lo(n)
            pool_.wait_ge(S["consts_done"], 8)
            for h in range(HEADS):
                slab_lo(4 * h + 4)
                right_sides(h)
                slab_lo(4 * h + 5)
                pool_.wait_ge(S["gam_done"], h + 1)
                if h:
                    pool_.wait_ge(S["aqk_done"], h)
                pool_.tensor_tensor(b3(gti), b3(gam[:, 1, :]), bm(m_le[:, :]), ALU.mult)\
                    .then_inc(S["gti_done"], 1)
                pool_.tensor_tensor(b3(gam[:, 0, :]), b3(gam[:, 0, :]), bm(m_pair[:, :]), ALU.mult)\
                    .then_inc(S["g1_done"], 1)
                pool_.wait_ge(S["g1_done"], 2 * h + 1)
                pool_.tensor_tensor(b3(gam[:, 0, :]), b3(gam[:, 0, :]), bc(beta[:, h, :], CHUNK),
                                    ALU.mult).then_inc(S["g1_done"], 1)
                for lv in range(LEVELS):
                    pool_.wait_ge(S["lt_done"], h + 1)
                    if lv >= 2:
                        pool_.wait_ge(S["t1_mm"], LEVELS * h + lv - 1)
                    else:
                        pool_.wait_ge(S["beta_mm"], h + 1)
                    pool_.tensor_tensor(b3(bt[lv % 2]), b3(ltT), bm(m_level[:, lv + 1, :]), ALU.mult)\
                        .then_inc(S["bt_done"], 1)
                    if lv == 1:
                        slab_lo(4 * h + 6)
                slab_lo(4 * h + 7)

            def ffn_lo(n, slot, ring):
                pool_.wait_ge(S["ffn_hi"], n)
                pool_.tensor_tensor(ring_lo[ring], stage[:, slot, :], ring_hi[ring].bitcast(F32),
                                    ALU.subtract).then_inc(S["ffn_lo"], 1)

            def act_lo_of(n, e, slot):
                pool_.wait_ge(S["act_hi_done"], n)
                pool_.tensor_tensor(act_lo[:, slot, :], up_conv[:, e, 0, :],
                                    act_hi[:, slot, :].bitcast(F32), ALU.subtract)\
                    .then_inc(S["act_lo_done"], 1)

            for n in range(4):
                ffn_lo(n + 1, n % 2, n % 3)
            act_lo_of(1, 0, 0)
            act_lo_of(2, 1, 1)
            with pool_.Fori(0, (FG - 1) // 2) as m:
                for b in range(2):
                    par = (1 + b) % 2
                    for n in range(6):
                        if n == 5:
                            act_lo_of(m * 4 + (2 * b + 3), 0, 2 * par)
                        ffn_lo(m * 12 + (4 + 6 * b + n + 1), n % 2, (1 + n) % 3)
                    act_lo_of(m * 4 + (2 * b + 4), 1, 2 * par + 1)
            for e in range(2):
                ffn_lo(4 + 6 * (FG - 1) + e + 1, e, (1 + e) % 3)

        @block.scalar
        def _(act):
            act.dma_start(norm_row[:, :], norm1_w.to_broadcast([P, D])).then_inc(S["norm_row_in"], 16)
            act.dma_start(wba[:, :, :], w_in_k[:, :, 4 * DN:4 * DN + 2 * HEADS])\
                .then_inc(S["ba_w_in"], 16)
            act.preload_act_table_set(LN_EXP_SET)

            def rstd(n, t):
                if n >= 2:
                    act.wait_ge(S["normed_T"], n - 1)
                act.activation(normed[:, n % 2, :], res[:, t, :], ACT.Square,
                               accum_out=stats[:, 0, t:t + 1]).then_inc(S["sq_done"], 1)
                act.wait_ge(S["sq_done"], n + 1)
                act.activation(stats[:, 1, t:t + 1], stats[:, 0, t:t + 1], ACT.Ln,
                               scale=1.0 / D, bias=eps_b[:, :]).then_inc(S["ln_done"], 1)
                act.wait_ge(S["ln_done"], n + 1)
                act.activation(stats[:, 2, t:t + 1], stats[:, 1, t:t + 1], ACT.Exp, scale=-0.5)\
                    .then_inc(S["rstd_done"], 1)

            def h_hi(n, t, dst, b):
                act.wait_ge(S["normed_T"], n + 1)
                act.activation(dst[:, :, t * P:(t + 1) * P], b3(bank(b, 2), P), ACT.Copy)\
                    .then_inc(S["h_hi"], 1)

            def slab_hi(n):
                act.wait_ge(stage_in[n % 2], 16 * (n // 2 + 1))
                if n >= 2:
                    act.wait_ge(S["dense_done"], slab_used(n - 2))
                act.activation(ring_hi[n % 2], stage[:, n % 2, :], ACT.Copy).then_inc(S["slab_hi"], 1)

            evacuated = [0]

            def evacuate_to(n):
                while evacuated[0] < n:
                    g = evacuated[0]
                    kind, i, j, half = GROUPS[g]
                    act.wait_ge(S["dense_done"], g + 1)
                    src = bank(g % 2)
                    gp = PG - 1 - j
                    to_cat = cat[:, 4 * half:4 * half + 4, i if kind == "proj" else HEADS + gp, :]
                    if kind == "lin":
                        act.wait_ge(S["cols_done"], 2)
                        act.activation(to_cat, b3(src, P), ACT.Identity, scale=cols[:, 9, gp:gp + 1],
                                       bias=pool_bias[:, gp:gp + 1]).then_inc(S["dense_evac"], 1)
                    elif i < HEADS and j == 3:
                        if half == 0:
                            silu(i, 0)
                            silu(i, 1)
                        act.activation(to_cat, b3(src, P), ACT.Silu).then_inc(S["dense_evac"], 1)
                        if half == 1:
                            silu(i, 2)
                    else:
                        if i < HEADS:
                            if i:
                                act.wait_ge(S["conv_step"], 12 * (i - 1) + 4 * (j + 1))
                            dst = raw[:, j, half * HALF:(half + 1) * HALF]
                        else:
                            act.wait_ge(S["conv_step"], 12 * HEADS)
                            if j >= 2:
                                act.wait_ge(S["dense_done"], INDEX[("lin", HEADS, j - 2, 1)] + 1)
                            dst = raw[:, j % 2, half * HALF:(half + 1) * HALF]
                        act.activation(dst, src, ACT.Copy).then_inc(S["dense_evac"], 1)
                    evacuated[0] += 1
                    if kind == "proj" and half == 1 and 4 * i + j + 2 < N_IN:
                        slab_hi(4 * i + j + 2)

            def silu(i, j):
                act.wait_ge(S["conv_step"], 12 * i + 4 * (j + 1))
                act.activation(qkv[:, j, :], qkv[:, j, :], ACT.Silu).then_inc(S["silu_done"], 1)

            act.wait_ge(S["eps_done"], 2)
            for t in range(TT):
                act.wait_ge(x_in[t], 16)
                rstd(t, t)
                if t:
                    h_hi(t - 1, t - 1, a_hi, 2 + 2 * ((t - 1) % 2))
                if t == 3:
                    slab_hi(0)
                elif t == 4:
                    slab_hi(1)
                elif t == 7:
                    evacuate_to(1)
            h_hi(TT - 1, TT - 1, a_hi, 2 + 2 * ((TT - 1) % 2))
            evacuate_to(2)
            act.wait_ge(S["cols_T"], 1)
            act.activation(cols[:, :, :].rearrange("p a b -> p (a b)"), bank(6)[:, 0:484], ACT.Copy)\
                .then_inc(S["cols_done"], 1)
            evacuate_to(3)
            act.wait_ge(S["ba_done"], 1)
            act.activation(sc[:, 0, :, :], ba[:, 0:HEADS, :], ACT.Exp, scale=-1.0)\
                .then_inc(S["sc_act"], 1)
            act.wait_ge(S["par_in"], 32)
            act.activation(decay_par[:, 2, :], decay_par[:, 0, :], ACT.Exp).then_inc(S["sc_act"], 1)
            act.wait_ge(S["sc_dve"], 3)
            act.activation(sc[:, 2, :, :], sc[:, 2, :, :], ACT.Exp).then_inc(S["sc_act"], 1)
            act.wait_ge(S["sc_dve"], 4)
            act.activation(sc[:, 3, :, :], sc[:, 4, :, :], ACT.Ln).then_inc(S["sc_act"], 1)
            act.wait_ge(S["cum_mm"], 1)
            act.activation(ex[:, :, :, :].rearrange("p a h b -> p (a h b)"),
                           bank(6)[:, 0:4 * HEADS * TT], ACT.Exp).then_inc(S["ex_done"], 1)

            def square_o(h):
                act.wait_ge(S["o_evac"], 2 * (h + 1))
                act.wait_ge(S["v_new_done"], NCH * (h + 1))
                act.activation(v_tok, o_T, ACT.Square).then_inc(S["sqo_done"], 1)

            def norm_o(h):
                act.wait_ge(S["sumsq_o_mm"], h + 1)
                act.activation(v_tok, bank(6, 2), ACT.Ln, scale=1.0 / P, bias=eps_b[:, :])\
                    .then_inc(S["ln_o"], 1)
                act.wait_ge(S["ln_o"], h + 1)
                act.activation(v_tok, v_tok, ACT.Exp, scale=-0.5).then_inc(S["r_o"], 1)

            for i in range(HEADS + 1):
                h = i - 1
                if h >= 0:
                    for s, (step, _) in enumerate(STEPS):
                        if s >= 2:
                            evacuate_to(groups_done(i, s))
                        if step == "start":
                            act.preload_act_table_set(LN_EXP_SET)
                            act.wait_ge(S["silu_done"], 3 * h + 3)
                            if h:
                                act.wait_ge(S["o_mm"], 2 * h)
                            act.activation(k_be, qkv[:, 0, :], ACT.Square).then_inc(S["sumsq_in"], 1)
                            act.activation(k_d, qkv[:, 1, :], ACT.Square).then_inc(S["sumsq_in"], 1)
                        elif step == "sumsq_q":
                            if h:
                                square_o(h - 1)
                            act.wait_ge(S["sumsq_q_mm"], h + 1)
                            act.activation(k_be, bank(4, 2), ACT.Ln, bias=eps_b[:, :])\
                                .then_inc(S["lnq"], 1)
                            act.wait_ge(S["lnq"], h + 1)
                            act.activation(k_be, k_be, ACT.Exp, scale=-0.5, bias=bias_q[:, :])\
                                .then_inc(S["rq"], 1)
                        elif step == "norm_o":
                            if h:
                                norm_o(h - 1)
                        elif step == "sumsq_k":
                            act.wait_ge(S["sumsq_k_mm"], h + 1)
                            act.activation(k_d, bank(2, 2), ACT.Ln, bias=eps_b[:, :])\
                                .then_inc(S["lnk"], 1)
                            act.wait_ge(S["lnk"], h + 1)
                            act.activation(k_d, k_d, ACT.Exp, scale=-0.5).then_inc(S["rk"], 1)
                        elif step == "decay":
                            act.wait_ge(S["decay_mm"], h + 1)
                            if h:
                                act.wait_ge(S["l1_done"], h)
                            act.activation(gam[:, :, :].rearrange("p a n -> p (a n)"), bank(4, 2), ACT.Exp)\
                                .then_inc(S["gam_done"], 1)
                        elif step == "decay_row":
                            act.wait_ge(S["decay_row_mm"], h + 1)
                            if h:
                                act.wait_ge(S["on_done"], h)
                                act.wait_ge(S["head_done"], h)
                            act.activation(o_T, bank(2, 2), ACT.Exp).then_inc(S["erow_done"], 1)
                        elif step.startswith("level") and step.endswith("a"):
                            lv = int(step[5])
                            act.wait_ge(S["t1_mm"], LEVELS * h + lv + 1)
                            act.activation(t1, bank(2), ACT.Copy).then_inc(S["t1_evac"], 1)
                        elif step == "u":
                            act.wait_ge(S["u_mm"], h + 1)
                            act.activation(v_tok, bank(2, 2), ACT.Copy).then_inc(S["u_evac"], 1)
                        elif step == "w":
                            act.wait_ge(S["w_mm"], h + 1)
                            act.activation(wT, bank(4, 2), ACT.Copy).then_inc(S["w_evac"], 1)
                        elif step.startswith("chunk") and step.endswith("b"):
                            c = int(step[5:-1])
                            if c % 8 == 7:
                                q = c // 8
                                act.wait_ge(S["o_mm"], 2 * h + q + 1)
                                act.wait_ge(S["qg_done"], h + 1)
                                act.activation(o_T[:, q * HALF:(q + 1) * HALF], bank(o_bank(c)), ACT.Copy)\
                                    .then_inc(S["o_evac"], 1)
                evacuate_to(PASS_START[i + 1] if i < HEADS else NG)
            square_o(HEADS - 1)
            norm_o(HEADS - 1)

            def split_cat(t):
                if t >= 2:
                    act.wait_ge(S["res_mm"], 2 * (t - 1))
                act.activation(ring_hi[t % 2], res[:, t, :], ACT.Copy).then_inc(S["ot_hi"], 1)

            act.wait_ge(S["dense_done"], NG)
            act.wait_ge(S["dense_evac"], NG)
            act.wait_ge(stage_in[0], 16 * (N_IN // 2 + 1))
            act.activation(a_hi[:, 0, :], stage[:, 0, :], ACT.Copy).then_inc(S["wo_hi"], 1)
            act.wait_ge(S["head_done"], HEADS)
            split_cat(0)
            for k in range(1, KT):
                act.wait_ge(stage_in[k % 2], 16 * (N_IN // 2 + k // 2 + 1))
                act.activation(a_hi[:, k, :], stage[:, k % 2, :], ACT.Copy).then_inc(S["wo_hi"], 1)
            split_cat(1)

            for t in range(TT):
                act.wait_ge(S["res_add"], 2 * (t + 1))
                rstd(TT + t, t)
                if t + 2 < TT:
                    split_cat(t + 2)
                if t:
                    h_hi(TT + t - 1, t - 1, h2_hi, 4 + 2 * ((t - 1) % 2))
            h_hi(2 * TT - 1, TT - 1, h2_hi, 4 + 2 * ((TT - 1) % 2))
            act.preload_act_table(ACT.Silu)

            def ffn_hi(arrivals, slot, ring, free, free_at):
                act.wait_ge(stage_in[slot], arrivals)
                act.wait_ge(free, free_at)
                act.activation(ring_hi[ring], stage[:, slot, :], ACT.Copy).then_inc(S["ffn_hi"], 1)

            def evacuate_up(n, e, gu, half, conv_at):
                act.wait_ge(S["up_mm"], n)
                if conv_at is not None:
                    act.wait_ge(S["up_conv_step"], conv_at)
                act.activation(up_raw[:, e, gu, half * HALF:(half + 1) * HALF],
                               bank(2 * gu + half), ACT.Copy).then_inc(S["raw_evac"], 1)

            def gate_silu(e, steps):
                act.wait_ge(S["up_conv_step"], steps)
                act.activation(up_conv[:, e, 0, :], up_conv[:, e, 0, :], ACT.Silu)\
                    .then_inc(S["gate_silu"], 1)

            def split_act(e, acts, slot, down_at):
                act.wait_ge(S["act_done"], acts)
                if down_at is not None:
                    act.wait_ge(S["res_mm"], down_at)
                act.activation(act_hi[:, slot, :], up_conv[:, e, 0, :], ACT.Copy)\
                    .then_inc(S["act_hi_done"], 1)

            for n in range(3):
                ffn_hi(STAGED + 16 * (n // 2 + 1), n % 2, n % 3, S["normed_T"], 2 * TT)
            for half in range(2):
                evacuate_up(half + 1, 0, 0, half, None)
            ffn_hi(STAGED + 32, 1, 0, S["up_mm"], 2)
            for n in range(2, 6):
                evacuate_up(n + 1, n // 4, (n // 2) % 2, n % 2, None)
            gate_silu(0, 3)
            split_act(0, 1, 0, None)
            for n in range(6, 8):
                evacuate_up(n + 1, 1, 1, n % 2, None)
            gate_silu(1, 9)
            split_act(1, 2, 1, None)
            with act.Fori(0, (FG - 1) // 2) as m:
                for b in range(2):
                    par = (1 + b) % 2

                    def at(n):
                        return m * 16 + (8 * (1 + b) + n)

                    def staged(n):
                        return m * (16 * 6) + (STAGED + 16 * ((4 + 6 * b + n) // 2 + 1))

                    def ups(n):
                        e, gu, half = n // 4, (n // 2) % 2, n % 2
                        evacuate_up(at(n + 1), e, gu, half, m * 24 + (12 * b + 6 * e + 3 * gu + 3))

                    ffn_hi(staged(0), 0, 1, S["up_mm"], at(0))
                    ffn_hi(staged(1), 1, 2, S["res_mm"], m * 32 + 16 * (b + 1))
                    ups(0)
                    ffn_hi(staged(2), 0, 0, S["res_mm"], m * 32 + 16 * (b + 1))
                    ups(1)
                    ffn_hi(staged(3), 1, 1, S["up_mm"], at(2))
                    ups(2)
                    ups(3)
                    ffn_hi(staged(4), 0, 2, S["up_mm"], at(4))
                    gate_silu(0, m * 24 + (12 * b + 15))
                    ups(4)
                    split_act(0, m * 4 + (2 * b + 3), 2 * par, m * 32 + 16 * (b + 1))
                    ups(5)
                    ffn_hi(staged(5), 1, 0, S["up_mm"], at(6))
                    ups(6)
                    gate_silu(1, m * 24 + (12 * b + 21))
                    ups(7)
                    split_act(1, m * 4 + (2 * b + 4), 2 * par + 1, m * 32 + 16 * (b + 1))
            last = 4 + 6 * (FG - 1)
            ffn_hi(STAGED + 16 * (last // 2 + 1), 0, 1, S["up_mm"], 8 * FG)
            ffn_hi(STAGED + 16 * (last // 2 + 1), 1, 2, S["res_mm"], 16 * FG)
            act.preload_act_table_set(LN_EXP_SET)
            for t in range(TT):
                act.wait_ge(S["res_add"], 2 * TT * FG + 2 * (t + 1))
                act.activation(up_raw[:, 0, 0, :], res[:, t, :], ACT.Square,
                               accum_out=stats[:, 0, t:t + 1]).then_inc(S["final_sq"], 1)
                act.wait_ge(S["final_sq"], t + 1)
                act.activation(stats[:, 1, t:t + 1], stats[:, 0, t:t + 1], ACT.Ln,
                               scale=1.0 / D, bias=eps_b[:, :]).then_inc(S["final_ln"], 1)
                act.wait_ge(S["final_ln"], t + 1)
                act.activation(stats[:, 2, t:t + 1], stats[:, 1, t:t + 1], ACT.Exp, scale=-0.5)\
                    .then_inc(S["final_r"], 1)

        @block.vector
        def _(dve):
            dve.memset(eps_b[:, :], EPS).then_inc(S["eps_done"], 1)
            dve.memset(bias_q[:, :], -0.5 * float(np.log(P))).then_inc(S["eps_done"], 1)
            dve.wait_ge(S["iota_done"], 4)
            dve.tensor_tensor(m_le[:, :], row_i[:, :], col_i[:, :], ALU.is_le).then_inc(S["cmp_done"], 1)
            dve.tensor_tensor(m_gt[:, :], row_i[:, :], col_i[:, :], ALU.is_gt).then_inc(S["cmp_done"], 1)
            dve.tensor_tensor(m_lt[:, :], row_i[:, :], col_i[:, :], ALU.is_lt).then_inc(S["cmp_done"], 1)
            dve.tensor_tensor(m_eq[:, :], row_i[:, :], col_i[:, :], ALU.is_equal)\
               .then_inc(S["cmp_done"], 1)
            dve.tensor_tensor(xor_i[:, :], row_i[:, :], col_i[:, :], ALU.bitwise_xor)\
               .then_inc(S["cmp_done"], 1)
            dve.tensor_scalar(inv_pos[:, :], col_i[:, 0:16], 1.0, None, ALU.add)\
               .then_inc(S["cmp_done"], 1)
            for m in (tri, suf, blk_ones, half_ones):
                dve.memset(m[:], 0.0).then_inc(S["mask_done"], 1)
            dve.memset(ones[:, :], 1.0).then_inc(S["mask_done"], 1)
            dve.wait_ge(S["cmp_done"], 6)
            for k in range(6):
                dve.tensor_scalar(shift_i[:, k, :], xor_i[:, :], k, None, ALU.logical_shift_right)\
                   .then_inc(S["cmp_done"], 1)
            dve.reciprocal(inv_pos[:, :], inv_pos[:, :]).then_inc(S["cmp_done"], 1)
            dve.wait_ge(S["cmp_done"], 13)
            for k in range(6):
                dve.scalar_tensor_tensor(m_level[:, k, :], shift_i[:, k, :], 1.0, m_lt[:, :],
                                         ALU.is_equal, ALU.mult).then_inc(S["mask_done"], 1)
            dve.scalar_tensor_tensor(m_pair[:, :], shift_i[:, 0, :], 1.0, m_gt[:, :],
                                     ALU.is_equal, ALU.mult).then_inc(S["mask_done"], 1)
            dve.wait_ge(S["mask_done"], 12)
            for par in range(2):
                r = rows_of(par)
                dve.tensor_copy(tri[r, r], m_le[r, :]).then_inc(S["consts_done"], 1)
                dve.tensor_copy(suf[r, r], m_gt[r, :]).then_inc(S["consts_done"], 1)
                dve.memset(blk_ones[r, r], 1.0).then_inc(S["consts_done"], 1)
                dve.memset(half_ones[r, par, :], 1.0).then_inc(S["consts_done"], 1)
            dve.wait_ge(S["ba_w_in"], 16)
            dve.tensor_copy(wba_hi[:, :, :], wba[:, :, :]).then_inc(S["ba_w_split"], 1)
            dve.wait_ge(S["ba_w_split"], 1)
            dve.tensor_tensor(wba_lo[:, :, :], wba[:, :, :], wba_hi[:, :, :].bitcast(F32), ALU.subtract)\
               .then_inc(S["ba_w_split"], 1)

            def norm(n, t):
                dve.wait_ge(S["rstd_done"], n + 1)
                dve.scalar_tensor_tensor(normed[:, n % 2, :], res[:, t, :], stats[:, 2, t:t + 1],
                                         norm_row[:, :], ALU.mult, ALU.mult)\
                   .then_inc(S["normed_done"], 1)

            def h_lo(n, t, hi, lo, b):
                dve.wait_ge(S["h_hi"], n + 1)
                c = slice(t * P, (t + 1) * P)
                dve.tensor_tensor(lo[:, :, c], b3(bank(b, 2), P), hi[:, :, c].bitcast(F32), ALU.subtract)\
                   .then_inc(S["h_lo"], 1)

            dve.wait_ge(S["norm_row_in"], 16)
            for t in range(TT):
                norm(t, t)
                if t:
                    h_lo(t - 1, t - 1, a_hi, a_lo, 2 + 2 * ((t - 1) % 2))
                if t == 6:
                    dve.wait_ge(S["ba_mm"], 1)
                    dve.tensor_copy(ba_T[:, 0:HALF], bank(6)[0:8, :]).then_inc(S["ba_evac"], 1)
            h_lo(TT - 1, TT - 1, a_hi, a_lo, 2 + 2 * ((TT - 1) % 2))

            dve.wait_ge(S["ba_mm"], 2)
            dve.tensor_copy(ba_T[:, HALF:SEQ], bank(7)[0:8, :]).then_inc(S["ba_evac"], 1)
            dve.wait_ge(S["ba_T_mm"], 1)
            dve.tensor_copy(ba[:, :, :], bank(7)[:, 0:8 * TT].rearrange("p (b c) -> p c b", c=8))\
               .then_inc(S["ba_done"], 1)
            dve.wait_ge(S["ba_done"], 1)
            dve.wait_ge(S["par_in"], 32)
            dve.tensor_tensor(sc[:, 1, :, :], ba[:, HEADS:2 * HEADS, :],
                              decay_par[:, 1, :].unsqueeze(2).to_broadcast([P, HEADS, TT]), ALU.add)\
               .then_inc(S["sc_dve"], 1)
            dve.wait_ge(S["sc_dve"], 1)
            dve.tensor_scalar(sc[:, 2, :, :], sc[:, 1, :, :], -1.0, None, ALU.mult)\
               .then_inc(S["sc_dve"], 1)
            dve.wait_ge(S["sc_dve"], 2)
            dve.tensor_tensor(sc[:, 2, :, :], sc[:, 1, :, :], sc[:, 2, :, :], ALU.min)\
               .then_inc(S["sc_dve"], 1)
            dve.wait_ge(S["sc_act"], 3)
            dve.tensor_scalar(sc[:, 4, :, :], sc[:, 2, :, :], 1.0, None, ALU.add)\
               .then_inc(S["sc_dve"], 1)
            dve.tensor_scalar(sc[:, 0, :, :], sc[:, 0, :, :], 1.0, None, ALU.add)\
               .then_inc(S["sc_dve"], 1)
            dve.wait_ge(S["sc_dve"], 5)
            dve.reciprocal(beta[:, :, :], sc[:, 0, :, :]).then_inc(S["sc_dve"], 1)
            dve.tensor_scalar(sc[:, 5, :, :], sc[:, 4, :, :], -1.0, None, ALU.add)\
               .then_inc(S["sc_dve"], 1)
            dve.wait_ge(S["sc_dve"], 7)
            dve.tensor_tensor(sc[:, 5, :, :], sc[:, 2, :, :], sc[:, 5, :, :], ALU.subtract)\
               .then_inc(S["sc_dve"], 1)
            dve.reciprocal(sc[:, 0, :, :], sc[:, 4, :, :]).then_inc(S["sc_dve"], 1)
            dve.tensor_scalar(sc[:, 1, :, :], sc[:, 1, :, :], 0.0, None, ALU.max)\
               .then_inc(S["sc_dve"], 1)
            dve.wait_ge(S["sc_dve"], 10)
            dve.tensor_tensor(sc[:, 5, :, :], sc[:, 5, :, :], sc[:, 0, :, :], ALU.mult)\
               .then_inc(S["sc_dve"], 1)
            dve.wait_ge(S["sc_dve"], 11)
            dve.tensor_tensor(sc[:, 1, :, :], sc[:, 1, :, :], sc[:, 5, :, :], ALU.add)\
               .then_inc(S["sc_dve"], 1)
            dve.wait_ge(S["sc_dve"], 12)
            dve.wait_ge(S["sc_act"], 4)
            dve.tensor_tensor(sc[:, 1, :, :], sc[:, 1, :, :], sc[:, 3, :, :], ALU.add)\
               .then_inc(S["sc_dve"], 1)
            dve.wait_ge(S["sc_dve"], 13)
            dve.scalar_tensor_tensor(g_tok[:, :, :], sc[:, 1, :, :], -1.0,
                                     decay_par[:, 2, :].unsqueeze(2).to_broadcast([P, HEADS, TT]),
                                     ALU.mult, ALU.mult).then_inc(S["sc_dve"], 1)
            dve.wait_ge(S["ex_done"], 1)
            dve.tensor_tensor(beg[:, :, :], beta[:, :, :], ex[:, 0, :, :], ALU.mult)\
               .then_inc(S["sc_dve"], 1)
            dve.wait_ge(S["sc_dve"], 15)
            dve.wait_ge(S["cols_done"], 1)
            dve.tensor_tensor(pool_bias[:, :], cols[:, 8, 0:PG], cols[:, 9, 0:PG], ALU.mult)\
               .then_inc(S["cols_done"], 1)

            conv_at = [0]

            def conv_op(i, seen):
                j, tap = divmod(conv_at[0] - 12 * i, 4)
                if j >= 3 or INDEX[("proj", i, j, 1)] >= seen:
                    return
                w = cols[:, 4 + (3 - tap), j * HEADS + i:j * HEADS + i + 1]
                if tap == 0:
                    dve.wait_ge(S["dense_evac"], INDEX[("proj", i, j, 1)] + 1)
                    dve.tensor_scalar(qkv[:, j, :], raw[:, j, :], w, None, ALU.mult)\
                       .then_inc(S["conv_step"], 1)
                else:
                    dve.wait_ge(S["conv_step"], conv_at[0])
                    dve.scalar_tensor_tensor(qkv[:, j, tap:SEQ], raw[:, j, 0:SEQ - tap], w,
                                             qkv[:, j, tap:SEQ], ALU.mult, ALU.add)\
                       .then_inc(S["conv_step"], 1)
                conv_at[0] += 1

            pool_at = [0, 0, 0]
            gam_flat = gam[:, :, :].rearrange("p a n -> p (a n)")

            def pool_op(seen):
                j, n, done = pool_at
                if j >= PG or INDEX[("proj", HEADS, j, 1)] >= seen:
                    return
                u = raw[:, j % 2, :]
                src = u if n == 0 else (raw[:, 2, :], gam_flat)[(n - 1) % 2]
                dst = (raw[:, 2, :], gam_flat)[n % 2]
                lag = 1 << n
                if n == 0:
                    dve.wait_ge(S["dense_evac"], INDEX[("proj", HEADS, j, 1)] + 1)
                if done:
                    dve.wait_ge(S["pooled_step"], done)
                if n <= PG - 1 - j:
                    dve.tensor_copy(dst[:, 0:lag], src[:, 0:lag]).then_inc(S["pooled_step"], 1)
                    dve.tensor_tensor(dst[:, lag:SEQ], src[:, lag:SEQ], src[:, 0:SEQ - lag], ALU.add)\
                       .then_inc(S["pooled_step"], 1)
                    pool_at[:] = [j, n + 1, done + 2]
                else:
                    w = POOL_WINDOWS[PG - 1 - j]
                    dve.scalar_tensor_tensor(src[:, 0:w - 1], src[:, 0:w - 1], float(w),
                                             inv_pos[:, 0:w - 1], ALU.mult, ALU.mult)\
                       .then_inc(S["pooled_step"], 1)
                    dve.wait_ge(S["pooled_step"], done + 1)
                    dve.scalar_tensor_tensor(u, src, 1.0 / w, u, ALU.mult, ALU.subtract)\
                       .then_inc(S["pooled_step"], 1)
                    pool_at[:] = [j + 1, 0, done + 2]

            def fill(i, seen):
                if i < HEADS:
                    conv_op(i, seen)
                else:
                    pool_op(seen)

            def norm_o(h):
                dve.wait_ge(S["r_o"], h + 1)
                dve.tensor_tensor(o_T, o_T, v_tok, ALU.mult).then_inc(S["on_done"], 1)
                dve.wait_ge(S["on_done"], h + 1)
                dve.scalar_tensor_tensor(cat[:, :, h, :], b3(o_T, P), cols[:, 10, 0:1], cat[:, :, h, :],
                                         ALU.mult, ALU.mult).then_inc(S["head_done"], 1)

            for i in range(HEADS + 1):
                h = i - 1
                for s, (step, _) in enumerate(STEPS if h >= 0 else ()):
                    if step == "norm_o" and h:
                        norm_o(h - 1)
                    elif step == "vT":
                        dve.wait_ge(S["v_T_mm"], h + 1)
                        if h:
                            dve.wait_ge(S["on_done"], h)
                        dve.tensor_tensor(b3(v_tok, P), b3(bank(6, 2), P), bc(beta[:, h, :], P), ALU.mult)\
                           .then_inc(S["vb_done"], 1)
                    elif step == "sumsq_q":
                        dve.wait_ge(S["rq"], h + 1)
                        dve.tensor_tensor(qkv[:, 0, :], qkv[:, 0, :], k_be, ALU.mult)\
                           .then_inc(S["qn_done"], 1)
                    elif step == "sumsq_k":
                        dve.wait_ge(S["rk"], h + 1)
                        dve.tensor_tensor(qkv[:, 1, :], qkv[:, 1, :], k_d, ALU.mult)\
                           .then_inc(S["kn_done"], 1)
                    elif step == "beta_kk":
                        dve.wait_ge(S["gti_done"], h + 1)
                        dve.wait_ge(S["beta_mm"], h + 1)
                        dve.tensor_tensor(gam[:, 1, :], gam[:, 1, :], bank(4), ALU.mult)\
                           .then_inc(S["gtb_done"], 1)
                        dve.wait_ge(S["gtb_done"], h + 1)
                        dve.wait_ge(S["kk_mm"], h + 1)
                        dve.tensor_tensor(ltT, bank(5), gam[:, 1, :], ALU.mult).then_inc(S["lt_done"], 1)
                        dve.wait_ge(S["g1_done"], 2 * h + 2)
                        dve.tensor_tensor(tmp, bank(5), gam[:, 0, :], ALU.mult)\
                           .then_inc(S["l1_done"], 1)
                        dve.wait_ge(S["l1_done"], h + 1)
                        dve.tensor_tensor(b3(xinv), bm(m_eq[:, :]), b3(tmp), ALU.subtract)\
                           .then_inc(S["x_upd"], 1)
                        dve.wait_ge(S["lt_done"], h + 1)
                        dve.wait_ge(S["x_upd"], LEVELS * h + 1)
                        dve.tensor_tensor(b3(tmp), b3(ltT), bm(m_level[:, 0, :]), ALU.mult)\
                           .then_inc(S["tmpt_done"], 1)
                        dve.wait_ge(S["tmpt_done"], h + 1)
                        dve.tensor_tensor(b3(xinvT), bm(m_eq[:, :]), b3(tmp), ALU.subtract)\
                           .then_inc(S["xt_upd"], 1)
                    elif step == "qk":
                        dve.wait_ge(S["qk_mm"], h + 1)
                        dve.tensor_tensor(aqkT, bank(2), gti, ALU.mult).then_inc(S["aqk_done"], 1)
                        dve.wait_ge(S["erow_done"], h + 1)
                        dve.tensor_tensor(qg.rearrange("p (b a n) -> p b a n", a=2, n=CHUNK),
                                          qkv[:, 0, :].rearrange("p (b a n) -> p b a n", a=2, n=CHUNK),
                                          o_T.rearrange("p (a b n) -> p b a n", a=2, n=CHUNK), ALU.mult)\
                           .then_inc(S["qg_done"], 1)
                    elif step == "kT":
                        dve.wait_ge(S["k_T_mm"], h + 1)
                        dve.tensor_tensor(b3(k_be, P), b3(bank(4, 2), P), bc(beg[:, h, :], P), ALU.mult)\
                           .then_inc(S["kbe_done"], 1)
                        dve.tensor_tensor(b3(k_d, P), b3(bank(4, 2), P), bc(ex[:, 1, h, :], P), ALU.mult)\
                           .then_inc(S["kd_done"], 1)
                    elif step.startswith("level") and step.endswith("b"):
                        lv = int(step[5])
                        if lv < LEVELS - 1:
                            dve.wait_ge(S["x_mm"], (LEVELS - 1) * h + lv + 1)
                            dve.tensor_tensor(xinv, xinv, bank(3), ALU.subtract).then_inc(S["x_upd"], 1)
                        dve.wait_ge(S["xt_mm"], LEVELS * h + lv + 1)
                        dve.tensor_tensor(xinvT, xinvT, bank(4), ALU.subtract).then_inc(S["xt_upd"], 1)
                        fill(i, groups_done(i, s - 1))
                    elif step == "w":
                        if h:
                            dve.wait_ge(S["s_upd"], (NCH + 1) * h)
                        dve.memset(state, 0.0).then_inc(S["s_upd"], 1)
                        fill(i, groups_done(i, s - 1))
                    elif step.startswith("chunk"):
                        c = int(step[5:-1])
                        r, blk = rows_of(c % 2), c // 2
                        if step.endswith("a"):
                            dve.wait_ge(S["v_mm"], NCH * h + c + 1)
                            if c == 0:
                                dve.wait_ge(S["u_evac"], h + 1)
                            dve.tensor_tensor(v_new[r, :], v_tok[r, blk * P:(blk + 1) * P],
                                              bank(6)[r, 0:P], ALU.subtract).then_inc(S["v_new_done"], 1)
                        else:
                            dve.wait_ge(S["s_mm"], NCH * h + c + 1)
                            dve.wait_ge(S["s_upd"], (NCH + 1) * h + c + 1)
                            dve.scalar_tensor_tensor(state, state, ex[:, 2 + c % 2, h, blk:blk + 1],
                                                     bank(6)[:, P:2 * P], ALU.mult, ALU.add)\
                               .then_inc(S["s_upd"], 1)
                            fill(i, groups_done(i, s - 1))
                if i < HEADS:
                    while conv_at[0] < 12 * (i + 1):
                        conv_op(i, NG)
                else:
                    while pool_at[0] < PG:
                        pool_op(NG)
            norm_o(HEADS - 1)

            def ot_lo(t):
                dve.wait_ge(S["ot_hi"], t + 1)
                dve.tensor_tensor(ring_lo[t % 2], res[:, t, :], ring_hi[t % 2].bitcast(F32),
                                  ALU.subtract).then_inc(S["ot_lo"], 1)

            def wo_lo(k):
                dve.wait_ge(S["wo_hi"], k + 1)
                dve.tensor_tensor(a_lo[:, k, :], stage[:, k % 2, :], a_hi[:, k, :].bitcast(F32),
                                  ALU.subtract).then_inc(S["wo_lo"], 1)

            wo_lo(0)
            ot_lo(0)
            for k in range(1, KT):
                wo_lo(k)
            ot_lo(1)
            dve.wait_ge(S["norm_row_in"], 32)
            for t in range(TT):
                dve.wait_ge(x_in[t], 32)
                for n in range(2):
                    dve.wait_ge(S["res_mm"], 2 * t + n + 1)
                    c = slice(n * BANK, (n + 1) * BANK)
                    dve.tensor_tensor(res[:, t, c], res[:, t, c], bank(2 * (t % 2) + n), ALU.add)\
                       .then_inc(S["res_add"], 1)
                if t + 2 < TT:
                    ot_lo(t + 2)
                if t:
                    h_lo(TT + t - 1, t - 1, h2_hi, h2_lo, 4 + 2 * ((t - 1) % 2))
                norm(TT + t, t)
            h_lo(2 * TT - 1, TT - 1, h2_hi, h2_lo, 4 + 2 * ((TT - 1) % 2))

            def conv_up_op(n, e, gate_col, value_col, steps, evacs, tiles, lo_at):
                if n == 6:
                    dve.wait_ge(S["up_conv_step"], steps + 6)
                    dve.wait_ge(S["gate_silu"], tiles + 1)
                    dve.tensor_tensor(up_conv[:, e, 0, :], up_conv[:, e, 0, :], up_conv[:, e, 1, :],
                                      ALU.mult).then_inc(S["act_done"], 1)
                    return
                gu, tap = divmod(n, 3)
                col = (gate_col, value_col)[gu]
                y, z = up_conv[:, e, gu, :], up_raw[:, e, gu, :]
                if tap == 0:
                    dve.wait_ge(S["raw_evac"], evacs + (2 * gu + 2))
                    if gu == 0 and lo_at is not None:
                        dve.wait_ge(S["act_lo_done"], lo_at)
                    dve.tensor_scalar(y, z, cols[:, 2, col], cols[:, 3, col], ALU.mult, ALU.add)\
                       .then_inc(S["up_conv_step"], 1)
                else:
                    dve.wait_ge(S["up_conv_step"], steps + n)
                    dve.scalar_tensor_tensor(y[:, tap:SEQ], z[:, 0:SEQ - tap], cols[:, 2 - tap, col],
                                             y[:, tap:SEQ], ALU.mult, ALU.add)\
                       .then_inc(S["up_conv_step"], 1)

            def add_down(downs, idx):
                t, n = divmod(idx, 2)
                dve.wait_ge(S["res_mm"], downs + (idx + 1))
                c = slice(n * BANK, (n + 1) * BANK)
                dve.tensor_tensor(res[:, t, c], res[:, t, c], bank(4 + idx % 4), ALU.add)\
                   .then_inc(S["res_add"], 1)

            for e in range(2):
                for n in range(7):
                    conv_up_op(n, e, slice(e, e + 1), slice(FT + e, FT + e + 1), 6 * e, 4 * e, e,
                               e if e else None)
            with dve.Fori(0, (FG - 1) // 2) as m:
                for b in range(2):
                    def tile_op(n, e):
                        tile = 2 * (b + 1) + e
                        conv_up_op(n, e, bass.ds(m * 4 + tile, 1), bass.ds(m * 4 + (FT + tile), 1),
                                   m * 24 + 6 * tile, m * 16 + 4 * tile, m * 4 + tile,
                                   m * 4 + (tile - 1))

                    for n in range(7):
                        tile_op(n, 0)
                    for n in range(3):
                        tile_op(n, 1)
                    dve.wait_ge(S["res_add"], m * 32 + 16 * (b + 1))
                    for idx in range(16):
                        add_down(m * 32 + 16 * (b + 1), idx)
                        if idx % 2 == 0 and idx < 8:
                            tile_op(3 + idx // 2, 1)
            dve.wait_ge(S["res_add"], 16 * FG)

            def final(t):
                dve.wait_ge(S["final_r"], t + 1)
                dve.scalar_tensor_tensor(res[:, t, :], res[:, t, :], stats[:, 2, t:t + 1],
                                         norm_row[:, :], ALU.mult, ALU.mult)\
                   .then_inc(S["final_done"], 1)

            dve.wait_ge(S["norm_row_in"], 48)
            for t in range(TT):
                add_down(16 * FG, 2 * t)
                add_down(16 * FG, 2 * t + 1)
                if t:
                    final(t - 1)
            final(TT - 1)

        @block.tensor
        def _(pe):
            def transpose_tile(n, b):
                pe.wait_ge(S["normed_done"], n + 1)
                if n >= 2:
                    pe.wait_ge(S["h_lo"], n - 1)
                for k in range(KT):
                    last = pe.matmul(bank(b, 2)[:, k * P:(k + 1) * P], normed[:, n % 2, k * P:(k + 1) * P],
                                     ident[:, :], start=True, stop=True, is_transpose=True)
                last.then_inc(S["normed_T"], 1)

            def three(out_, l_hi, l_lo, r_hi, r_lo, first, final):
                pe.matmul(out_, l_hi, r_hi, start=first, stop=False)
                pe.matmul(out_, l_lo, r_hi, start=False, stop=False)
                return pe.matmul(out_, l_hi, r_lo, start=False, stop=final)

            at = [0, 0]

            def dense(n, only_pass=HEADS):
                for _ in range(n):
                    g, u = at
                    if g >= NG or GROUPS[g][1] > only_pass:
                        return
                    kind, i, j, half = GROUPS[g]
                    c = slice(half * HALF, (half + 1) * HALF)
                    if u == 0:
                        if g >= 2:
                            pe.wait_ge(S["dense_evac"], g - 1)
                        if kind == "proj":
                            pe.wait_ge(S["slab_lo"], 4 * i + j + 1)
                            if i == 0:
                                pe.wait_ge(S["h_lo"], 4 * (half + 1))
                        else:
                            pe.wait_ge(S["pool_w_in"], 16)
                            pe.wait_ge(S["pooled_step"], sum(2 * (PG - a) + 2 for a in range(j + 1)))
                    if kind == "lin":
                        last = pe.matmul(bank(g % 2), pool_wt[:, PG - 1 - j, :], raw[:, j % 2, c],
                                         start=True, stop=True)
                    else:
                        k, part = divmod(u, 3)
                        slot, ks = (4 * i + j) % 2, slice(k * P, (k + 1) * P)
                        w, a = ((ring_hi, a_hi), (ring_lo, a_hi), (ring_hi, a_lo))[part]
                        last = pe.matmul(bank(g % 2), w[slot][:, ks], a[:, k, c], start=(u == 0),
                                         stop=(u == UNITS[g] - 1))
                    at[1] += 1
                    if at[1] == UNITS[g]:
                        last.then_inc(S["dense_done"], 1)
                        at[:] = [g + 1, 0]

            def chunks(out_cols, l_of, r_of, done, banked):
                for b in range(TT):
                    for par in range(2):
                        last = pe.matmul(banked[rows_of(par), b * out_cols:(b + 1) * out_cols],
                                         l_of(par, b), r_of(par, b), start=True, stop=True)
                last.then_inc(S[done], 1)

            def blk64(ap):
                return lambda par, b: ap[rows_of(par), b * CHUNK:(b + 1) * CHUNK]

            def tok64(ap):
                return lambda par, b: ap[:, b * P + par * CHUNK:b * P + (par + 1) * CHUNK]

            def sum_of_squares(b, src, done):
                for half in range(2):
                    last = pe.matmul(bank(b + half), ones[:, :], src[:, half * HALF:(half + 1) * HALF],
                                     start=True, stop=True)
                last.then_inc(S[done], 1)

            def norm_o(h):
                pe.wait_ge(S["sqo_done"], h + 1)
                pe.wait_ge(S["s_upd"], (NCH + 1) * (h + 1))
                sum_of_squares(6, v_tok, "sumsq_o_mm")

            def gates(half):
                pe.wait_ge(S["h_lo"], 4 * (half + 1))
                c = slice(half * HALF, (half + 1) * HALF)
                for k in range(KT):
                    last = three(bank(6 + half)[0:8, :], wba_hi[:, k, :], wba_lo[:, k, :],
                                 a_hi[:, k, c], a_lo[:, k, c], k == 0, k == KT - 1)
                last.then_inc(S["ba_mm"], 1)

            pe.wait_ge(S["ident_done"], 2)
            for t in range(4):
                transpose_tile(t, 2 + 2 * (t % 2))
            pe.wait_ge(S["ba_w_split"], 2)
            gates(0)
            for t in range(4, TT):
                transpose_tile(t, 2 + 2 * (t % 2))
                dense(12, 0)
            gates(1)
            pe.wait_ge(S["rows_in"], 96)
            pe.wait_ge(S["ba_evac"], 1)
            for a in range(11):
                last = pe.matmul(bank(6)[:, 44 * a:44 * (a + 1)], rows[0:44, a, :], ident[0:44, 0:44],
                                 start=True, stop=True, is_transpose=True)
            last.then_inc(S["cols_T"], 1)
            dense(24, 0)
            pe.wait_ge(S["ba_evac"], 2)
            for t in range(TT):
                last = pe.matmul(bank(7)[:, 8 * t:8 * t + 8], ba_T[:, t * P:(t + 1) * P],
                                 ident[0:8, 0:8], start=True, stop=True, is_transpose=True)
            last.then_inc(S["ba_T_mm"], 1)
            dense(48, 0)
            pe.wait_ge(S["sc_dve"], 14)
            pe.wait_ge(S["cols_done"], 1)
            pe.wait_ge(S["consts_done"], 8)
            gs = g_tok[:, :, :].rearrange("p h b -> p (h b)")
            for n, m in enumerate((tri[:, :], suf[:, :], half_ones[:, 0, :], half_ones[:, 1, :])):
                last = pe.matmul(bank(6)[:, n * HEADS * TT:(n + 1) * HEADS * TT], m, gs, start=True,
                                 stop=True)
            last.then_inc(S["cum_mm"], 1)
            dense(10 ** 6, 0)
            for i in range(1, HEADS + 1):
                h = i - 1
                for step, filler in STEPS:
                    if step == "start":
                        pass
                    elif step == "norm_o":
                        if h:
                            norm_o(h - 1)
                    elif step == "sumsq_q":
                        pe.wait_ge(S["sumsq_in"], 2 * h + 1)
                        sum_of_squares(4, k_be, "sumsq_q_mm")
                    elif step == "vT":
                        if h:
                            pe.wait_ge(S["ln_o"], h)
                        pe.wait_ge(S["silu_done"], 3 * h + 3)
                        for b in range(TT):
                            last = pe.matmul(bank(6, 2)[:, b * P:(b + 1) * P], qkv[:, 2, b * P:(b + 1) * P],
                                             ident[:, :], start=True, stop=True, is_transpose=True)
                        last.then_inc(S["v_T_mm"], 1)
                    elif step == "sumsq_k":
                        pe.wait_ge(S["sumsq_in"], 2 * h + 2)
                        sum_of_squares(2, k_d, "sumsq_k_mm")
                    elif step == "decay":
                        pe.wait_ge(S["rhs_done"], 3 * h + 2)
                        pe.wait_ge(S["lnq"], h + 1)
                        pe.matmul(bank(4), tri[:, :], r1, start=True, stop=True)
                        pe.matmul(bank(5), suf[:, :], r2, start=True, stop=True)\
                          .then_inc(S["decay_mm"], 1)
                    elif step == "decay_row":
                        pe.wait_ge(S["lnk"], h + 1)
                        pe.matmul(bank(2), half_ones[:, 0, :], r2, start=True, stop=True)
                        pe.matmul(bank(3), half_ones[:, 1, :], r2, start=True, stop=True)\
                          .then_inc(S["decay_row_mm"], 1)
                    elif step == "beta_kk":
                        pe.wait_ge(S["gam_done"], h + 1)
                        pe.wait_ge(S["rhs_done"], 3 * h + 3)
                        pe.matmul(bank(4), blk_ones[:, :], r3, start=True, stop=True)\
                          .then_inc(S["beta_mm"], 1)
                        pe.wait_ge(S["kn_done"], h + 1)
                        chunks(CHUNK, tok64(qkv[:, 1, :]), tok64(qkv[:, 1, :]), "kk_mm", bank(5))
                    elif step == "qk":
                        pe.wait_ge(S["erow_done"], h + 1)
                        pe.wait_ge(S["qn_done"], h + 1)
                        chunks(CHUNK, tok64(qkv[:, 1, :]), tok64(qkv[:, 0, :]), "qk_mm", bank(2))
                    elif step == "kT":
                        pe.wait_ge(S["l1_done"], h + 1)
                        for b in range(TT):
                            last = pe.matmul(bank(4, 2)[:, b * P:(b + 1) * P], qkv[:, 1, b * P:(b + 1) * P],
                                             ident[:, :], start=True, stop=True, is_transpose=True)
                        last.then_inc(S["k_T_mm"], 1)
                    elif step.startswith("level") and step.endswith("a"):
                        lv = int(step[5])
                        pe.wait_ge(S["bt_done"], LEVELS * h + lv + 1)
                        pe.wait_ge(S["x_upd"], LEVELS * h + lv + 1)
                        if lv == 0:
                            pe.wait_ge(S["aqk_done"], h + 1)
                        chunks(CHUNK, blk64(bt[lv % 2]), blk64(xinv), "t1_mm", bank(2))
                    elif step.startswith("level"):
                        lv = int(step[5])
                        pe.wait_ge(S["t1_evac"], LEVELS * h + lv + 1)
                        pe.wait_ge(S["xt_upd"], (LEVELS + 1) * h + lv + 1)
                        if lv == 0:
                            pe.wait_ge(S["kd_done"], h + 1)
                        if lv < LEVELS - 1:
                            chunks(CHUNK, blk64(xinvT), blk64(t1), "x_mm", bank(3))
                        chunks(CHUNK, blk64(t1), blk64(xinvT), "xt_mm", bank(4))
                    elif step == "u":
                        pe.wait_ge(S["xt_upd"], (LEVELS + 1) * (h + 1))
                        pe.wait_ge(S["vb_done"], h + 1)
                        chunks(P, blk64(xinvT), lambda par, b: v_tok[rows_of(par), b * P:(b + 1) * P],
                               "u_mm", bank(2, 2))
                    elif step == "w":
                        for b in range(TT):
                            for par in range(2):
                                last = pe.matmul(bank(4 + par)[:, b * CHUNK:(b + 1) * CHUNK],
                                                 k_be[rows_of(par), b * P:(b + 1) * P],
                                                 blk64(xinvT)(par, b), start=True, stop=True)
                        last.then_inc(S["w_mm"], 1)
                    elif step.endswith("a"):
                        c = int(step[5:-1])
                        par, b = c % 2, c // 2
                        if c == 0:
                            pe.wait_ge(S["w_evac"], h + 1)
                        if c == 0 and h:
                            pe.wait_ge(S["o_evac"], 2 * h)
                        pe.wait_ge(S["s_upd"], (NCH + 1) * h + c + 1)
                        pe.matmul(bank(6)[rows_of(par), 0:P],
                                  wT[:, par * HALF + b * CHUNK:][:, 0:CHUNK], state, start=True,
                                  stop=True).then_inc(S["v_mm"], 1)
                        o_at = bank(o_bank(c))[:, (c % 8) * CHUNK:(c % 8 + 1) * CHUNK]
                        pe.matmul(o_at, state, tok64(qg)(par, b), start=True, stop=False)
                    else:
                        c = int(step[5:-1])
                        par, b = c % 2, c // 2
                        r = rows_of(par)
                        o_at = bank(o_bank(c))[:, (c % 8) * CHUNK:(c % 8 + 1) * CHUNK]
                        pe.wait_ge(S["v_new_done"], NCH * h + c + 1)
                        pe.matmul(bank(6)[:, P:2 * P], k_d[r, b * P:(b + 1) * P], v_new[r, :],
                                  start=True, stop=True).then_inc(S["s_mm"], 1)
                        last = pe.matmul(o_at, v_new[r, :], aqkT[r, b * CHUNK:(b + 1) * CHUNK],
                                         start=False, stop=True)
                        if c % 8 == 7:
                            last.then_inc(S["o_mm"], 1)
                    dense(filler, i)
                dense(10 ** 6, i)
            norm_o(HEADS - 1)

            for t in range(TT):
                pe.wait_ge(S["ot_lo"], t + 1)
                if t >= 2:
                    pe.wait_ge(S["res_add"], 2 * (t - 1))
                for n in range(2):
                    for k in range(KT):
                        if t == 0 and n == 0:
                            pe.wait_ge(S["wo_lo"], k + 1)
                        ks, c = slice(k * P, (k + 1) * P), slice(n * BANK, (n + 1) * BANK)
                        last = three(bank(2 * (t % 2) + n), ring_hi[t % 2][:, ks],
                                     ring_lo[t % 2][:, ks], a_hi[:, k, c], a_lo[:, k, c],
                                     k == 0, k == KT - 1)
                    last.then_inc(S["res_mm"], 1)
                if t:
                    transpose_tile(TT + t - 1, 4 + 2 * ((t - 1) % 2))
            transpose_tile(2 * TT - 1, 4 + 2 * ((TT - 1) % 2))

            def up(slabs, evacs, ring_at):
                for e in range(2):
                    for gu in range(2):
                        n = 2 * e + gu
                        ring = (ring_at + n) % 3
                        pe.wait_ge(S["ffn_lo"], slabs + (n + 1))
                        for half in range(2):
                            if evacs is not None or n >= 2:
                                pe.wait_ge(S["raw_evac"], (0 if evacs is None else evacs) +
                                           (2 * n + half - 3))
                            c = slice(half * HALF, (half + 1) * HALF)
                            for k in range(KT):
                                ks = slice(k * P, (k + 1) * P)
                                last = three(bank(2 * gu + half), ring_hi[ring][:, ks],
                                             ring_lo[ring][:, ks], h2_hi[:, k, c], h2_lo[:, k, c],
                                             k == 0, k == KT - 1)
                            last.then_inc(S["up_mm"], 1)

            def down(slabs, acts, adds, par, ring_at):
                pe.wait_ge(S["ffn_lo"], slabs)
                pe.wait_ge(S["act_lo_done"], acts)
                for idx in range(16):
                    t, n = divmod(idx, 2)
                    pe.wait_ge(S["res_add"], adds + (idx + 13))
                    ts_, c = slice(t * P, (t + 1) * P), slice(n * BANK, (n + 1) * BANK)
                    for e in range(2):
                        ring = (ring_at + e) % 3
                        last = three(bank(4 + idx % 4), act_hi[:, 2 * par + e, ts_],
                                     act_lo[:, 2 * par + e, ts_], ring_hi[ring][:, c],
                                     ring_lo[ring][:, c], e == 0, e == 1)
                    last.then_inc(S["res_mm"], 1)

            pe.wait_ge(S["h_lo"], 2 * TT)
            pe.wait_ge(S["res_add"], 16)
            up(0, None, 0)
            with pe.Fori(0, (FG - 1) // 2) as m:
                for b in range(2):
                    up(m * 12 + (4 + 6 * b), m * 16 + 8 * (1 + b), 1)
                    down(m * 12 + (10 + 6 * b), m * 4 + (2 + 2 * b), m * 32 + 16 * b, b, 2)
            down(4 + 6 * (FG - 1) + 2, 2 * FG, 16 * (FG - 1), (FG - 1) % 2, 1)


_INS = ["x", "norm1_w", "w_in", "conv_qkv_w", "a_log", "dt_bias", "onorm_w", "pool_w", "pool_b",
        "pool_scale", "w_out", "norm2_w", "w_up", "ffn_conv_w", "ffn_conv_b", "w_down",
        "final_norm_w"]


def kernel(**inputs):
    import concourse.bacc as bacc
    from concourse.bass_utils import run_bass_kernel_spmd

    nc = bacc.Bacc("TRN2", target_bir_lowering=False, num_devices=1)
    arrays, args = {}, []
    for name in _INS:
        a = np.ascontiguousarray(inputs[name])
        arrays[f"in_{name}"] = a
        args.append(nc.dram_tensor(f"in_{name}", a.shape, mybir.dt.from_np(a.dtype),
                                   kind="ExternalInput").ap())
    out = nc.dram_tensor("out_y", inputs["x"].shape, F32, kind="ExternalOutput").ap()
    block_program(nc, *args, out)
    r = run_bass_kernel_spmd(nc, [arrays], core_ids=[0])
    return r.results[0]["out_y"]
```

```python
from contextlib import ExitStack

import concourse.bass as bass
import numpy as np
from concourse import mybir

F32 = mybir.dt.float32
F32R = mybir.dt.float32r
I32 = mybir.dt.int32
ALU = mybir.AluOpType
ACT = mybir.ActivationFunctionType

P = 128
BANK = 512
CHUNK = 64
HEADS = 4
EPS = 1e-6
POOL_WINDOWS = (2, 4, 8, 16)
LN_EXP_SET = "natural_log_exp_and_others"
LEVELS = 5

CHUNK_FILL = ({"a": 5, "b": 3}, {"a": 2, "b": 2})
STEPS = ([("start", 3), ("sumsq_q", 3), ("sumsq_k", 6), ("decay", 3), ("norm_o", 5), ("decay_row", 3),
          ("vT", 4), ("beta_kk", 5), ("qk", 5), ("kT", 5)]
         + [s for lv in range(LEVELS) for s in ((f"level{lv}a", 5), (f"level{lv}b", 3))]
         + [("u", 4), ("w", 4)]
         + [(f"chunk{c}{ab}", CHUNK_FILL[c % 2][ab]) for c in range(16) for ab in "ab"])


def block_program(nc, x, norm1_w, w_in, conv_qkv_w, a_log, dt_bias, onorm_w, pool_w, pool_b,
                  pool_scale, w_out, norm2_w, w_up, ffn_conv_w, ffn_conv_b, w_down, final_norm_w, out):
    SEQ, D = x.shape[1], x.shape[2]
    KT = D // P
    TT = SEQ // P
    HALF = SEQ // 2
    DN = HEADS * P
    PG = len(POOL_WINDOWS)
    FT = w_down.shape[1] // P
    FG = FT // 2
    NCH = SEQ // CHUNK
    assert HALF == BANK and TT == 8 and FT % 2 == 0 and FG % 2 == 1

    x_t = x[0].rearrange("(t p) d -> t p d", p=P)
    out_t = out[0].rearrange("(t p) d -> t p d", p=P)
    w_in_k = w_in[0].rearrange("(k p) n -> p k n", p=P)
    w_up_k = w_up[0].rearrange("(k p) n -> p k n", p=P)
    w_out_k = w_out[0].rearrange("(k p) n -> k p n", p=P)
    w_down_k = w_down[0].rearrange("(f p) n -> f p n", p=P)

    def in_proj_column(i, j):
        return j * DN + i * P if i < HEADS else 4 * DN + 2 * HEADS + (PG - 1 - j) * P

    with ExitStack() as ctx:
        def sb(name, shape, dt=F32):
            return ctx.enter_context(nc.sbuf_tensor(name, shape, dt))

        def sem(name):
            return ctx.enter_context(nc.semaphore(name))

        a_hi = sb("a_hi", [P, KT, SEQ], F32R)
        with nc.sbuf_tensor("a_lo", [P, KT, SEQ], F32R) as a_lo:
            pass
        with ExitStack() as spare:
            spare_hi = spare.enter_context(nc.sbuf_tensor("spare_hi", [P, D], F32R))
            spare_lo = spare.enter_context(nc.sbuf_tensor("spare_lo", [P, D], F32R))
        mlp = sb("mlp", [P, 8 * SEQ])
        act_hi, act_lo = a_hi[:, 0:4, :], a_hi[:, 4:8, :]
        up_raw = mlp[:, 0:4 * SEQ].rearrange("p (e g t) -> p e g t", e=2, g=2)
        up_conv = mlp[:, 4 * SEQ:8 * SEQ].rearrange("p (e g t) -> p e g t", e=2, g=2)

        B_WORDS = 18432
        with ExitStack() as early:
            early.enter_context(nc.sbuf_tensor("early_gap", [P, 6 * SEQ], F32))
            rows = early.enter_context(nc.sbuf_tensor("rows", [P, 11, P], F32))
            col_i = early.enter_context(nc.sbuf_tensor("col_i", [P, CHUNK], I32))
            row_i = early.enter_context(nc.sbuf_tensor("row_i", [P, CHUNK], I32))
            xor_i = early.enter_context(nc.sbuf_tensor("xor_i", [P, CHUNK], I32))
            shift_i = early.enter_context(nc.sbuf_tensor("shift_i", [P, 6, CHUNK], I32))
            wba = early.enter_context(nc.sbuf_tensor("wba", [P, KT, 8], F32))
            wba_hi = early.enter_context(nc.sbuf_tensor("wba_hi", [P, KT, 8], F32R))
            wba_lo = early.enter_context(nc.sbuf_tensor("wba_lo", [P, KT, 8], F32R))
            ba_T = early.enter_context(nc.sbuf_tensor("ba_T", [8, SEQ], F32))
            ba = early.enter_context(nc.sbuf_tensor("ba", [P, 8, TT], F32))
            sc = early.enter_context(nc.sbuf_tensor("sc", [P, 6, HEADS, TT], F32))
        with ExitStack() as late:
            h2_hi = late.enter_context(nc.sbuf_tensor("h2_hi", [P, KT, SEQ], F32R))
            h2_lo = late.enter_context(nc.sbuf_tensor("h2_lo", [P, KT, SEQ], F32R))
            with nc.sbuf_tensor("normed", [P, 2, D], F32) as normed:
                pass
            ring2_hi = late.enter_context(nc.sbuf_tensor("ring2_hi", [P, D], F32R))
            ring2_lo = late.enter_context(nc.sbuf_tensor("ring2_lo", [P, D], F32R))
        dn_all = sb("dn_all", [P, B_WORDS])
        used = [0]

        def dn(words):
            used[0] += words
            assert used[0] <= B_WORDS
            return dn_all[:, used[0] - words:used[0]]

        raw = dn(3 * SEQ).rearrange("p (j t) -> p j t", j=3)
        qkv = dn(3 * SEQ).rearrange("p (j t) -> p j t", j=3)
        qg = dn(SEQ)
        wT = dn(SEQ)
        v_tok = dn(SEQ)
        xinv = dn(TT * CHUNK)
        xinvT = dn(TT * CHUNK)
        t1 = dn(TT * CHUNK)
        r1 = dn(TT * CHUNK)
        r3 = dn(TT * CHUNK)
        r2 = dn(TT * CHUNK)
        gam = dn(2 * TT * CHUNK).rearrange("p (a n) -> p a n", a=2)
        gti = dn(TT * CHUNK)
        tmp = dn(TT * CHUNK)
        state = dn(P)
        v_new = dn(P)
        k_be = dn(SEQ)
        k_d = dn(SEQ)
        o_T = dn(SEQ)
        aqkT = sb("aqkT", [P, TT, 2, CHUNK])
        bt = [r1, r3]
        ltT = r2
        gam_flat = gam[:, :, :].rearrange("p a n -> p (a n)")
        res = sb("res", [P, TT, D])
        cat = res[:, :, :].rearrange("p t (k n) -> p t k n", n=P)
        stage = sb("stage", [P, 2, D])
        ring_hi01 = sb("ring_hi01", [P, 2, D], F32R)
        ring_lo01 = sb("ring_lo01", [P, 2, D], F32R)
        ring_hi = [ring_hi01[:, 0, :], ring_hi01[:, 1, :], ring2_hi[:, :]]
        ring_lo = [ring_lo01[:, 0, :], ring_lo01[:, 1, :], ring2_lo[:, :]]
        SPARE = 3
        ring_hi.append(spare_hi[:, :])
        ring_lo.append(spare_lo[:, :])
        norm_row = sb("norm_row", [P, D])
        ident = sb("ident", [P, P])
        ones = sb("ones", [P, P])
        tri = sb("tri", [P, P])
        suf = sb("suf", [P, P])
        blk_ones = sb("blk_ones", [P, P])
        half_ones = sb("half_ones", [P, 2, P])
        m_le = sb("m_le", [P, CHUNK])
        m_gt = sb("m_gt", [P, CHUNK])
        m_lt = sb("m_lt", [P, CHUNK])
        m_eq = sb("m_eq", [P, CHUNK])
        m_pair = sb("m_pair", [P, CHUNK])
        m_level = sb("m_level", [P, 6, CHUNK])
        cols = sb("cols", [P, 11, 44])
        pool_wt = sb("pool_wt", [P, PG, P])
        pool_bias = sb("pool_bias", [P, PG])
        inv_pos = sb("inv_pos", [P, 16])
        decay_par = sb("decay_par", [P, 3, HEADS])
        beta = sb("beta", [P, HEADS, TT])
        g_tok = sb("g_tok", [P, HEADS, TT])
        beg = sb("beg", [P, HEADS, TT])
        ex = sb("ex", [P, 4, HEADS, TT])
        stats = sb("stats", [P, 3, TT])
        bias_q = sb("bias_q", [P, 1])
        eps_b = sb("eps_b", [P, 1])

        ps = ctx.enter_context(nc.psum_tensor("ps", [P, 8 * BANK], F32))

        def bank(b, n=1):
            return ps[:, b * BANK:(b + n) * BANK]

        x_in = [sem(f"x_in{t}") for t in range(TT)]
        stage_in = [sem(f"stage_in{s}") for s in range(2)]
        names = """rows_in ba_w_in par_in pool_w_in norm_row_in out_written
            iota_done cmp_done mask_done consts_done eps_done ident_done cols_T cols_done
            sq_done ln_done rstd_done normed_done normed_T h_hi h_lo ba_w_split ba_mm ba_evac ba_T_mm ba_done
            sc_act sc_dve cum_mm ex_done
            slab_hi slab_lo dense_done dense_evac
            conv_step silu_done pooled_step
            rhs_done sumsq_in sumsq_q_mm sumsq_k_mm v_T_mm vb_done lnq lnk rq rk qn_done kn_done
            decay_mm gam_done decay_row_mm erow_done gti_done g1_done beta_mm kk_mm qk_mm
            gtb_done lt_done l1_done x_upd xt_upd tmpt_done aqk_cleared aqk_done qg_done k_T_mm kbe_done kd_done
            bt_done t1_mm t1_evac x_mm xt_mm u_mm u_evac w_mm w_evac
            v_mm v_new_done s_mm s_upd o_mm o_evac sqo_done sumsq_o_mm ln_o r_o on_done head_done
            wo_hi wo_lo ot_hi ot_lo res_mm res_add
            ffn_hi ffn_lo up_mm raw_evac up_conv_step gate_silu act_done act_hi_done act_lo_done
            final_sq final_ln final_r final_done""".split()
        S = {n: sem(n) for n in names}

        block = ctx.enter_context(nc.Block())

        def bc(scalars, n):
            return scalars.unsqueeze(2).to_broadcast([P, scalars.shape[1], n])

        def bm(mask, n=TT):
            return mask.unsqueeze(1).to_broadcast([P, n, CHUNK])

        def b3(ap, n=CHUNK):
            return ap.rearrange("p (b n) -> p b n", n=n)

        def o_bank(c):
            return (7, 5)[c // 8]

        def out_bank(t, n):
            return 2 + 2 * t + n if t < 2 else 2 * (t % 2) + n

        def h2_bank(t):
            return 6 - 2 * (t % 2)

        def rows_of(par):
            return slice(CHUNK * par, CHUNK * par + CHUNK)

        GROUPS = [("proj", 0, j, h) for js in ((0, 1),) for h in range(2) for j in js]
        GROUPS += [("proj", i, j, h) for i in range(HEADS) for j in range(4) for h in range(2)
                   if i or j >= 2]
        pool = [[(kind, HEADS, j, h) for h in range(2)] for kind, j in
                (("proj", 0), ("proj", 1), ("lin", 0), ("proj", 2), ("lin", 1), ("proj", 3),
                 ("lin", 2), ("lin", 3))]
        GROUPS += [g for pair in pool for g in pair]
        INDEX = {g: n for n, g in enumerate(GROUPS)}
        NG = len(GROUPS)
        UNITS = [24 if g[0] == "proj" else 1 for g in GROUPS]
        PASS_START = [8 * i for i in range(HEADS + 1)]

        def groups_done(i, step):
            left, n = sum(f for _, f in STEPS[:step]), PASS_START[i]
            while n < NG and UNITS[n] <= left:
                left -= UNITS[n]
                n += 1
            return n

        def slab_used(n):
            return INDEX[("proj", n // 4, n % 4, 1)] + 1

        N_IN = 4 * (HEADS + 1)
        K_ORDER = list(range(HEADS - 1)) + list(range(KT - 1, HEADS - 2, -1))
        CAT_PARTS = [(0, HEADS - 1), (HEADS + 1, KT), (HEADS - 1, HEADS + 1)]
        SPLITS = 2 * len(CAT_PARTS)

        def part_of(k):
            return [lo <= k < hi for lo, hi in CAT_PARTS].index(True)

        def tile_split(t):
            return SPLITS - 1 + t

        def load_up(sp, g, e, gu):
            first = gu * FT * P + e * P
            src = w_up_k[:, :, bass.ds(g * (2 * P) + first, P)]
            sp.dma_start(stage[:, gu, :].rearrange("p (k n) -> p k n", n=P), src)\
              .then_inc(stage_in[gu], 16)

        def load_down(sp, f, slot):
            src = w_down[0, bass.ds(f * P, P), :]
            sp.dma_start(stage[:, slot, :], src).then_inc(stage_in[slot], 16)

        @block.sync
        def _(sp):
            def slab(n):
                if n >= 2:
                    sp.wait_ge(S["slab_lo"], n - 1)
                c = in_proj_column(n // 4, n % 4)
                sp.dma_start(stage[:, n % 2, :].rearrange("p (k n) -> p k n", n=P),
                             w_in_k[:, :, c:c + P]).then_inc(stage_in[n % 2], 16)

            for t in range(TT):
                sp.dma_start(res[:, t, :], x_t[t]).then_inc(x_in[t], 16)
                if t in (3, 4):
                    slab(t - 3)
            sp.dma_start(decay_par[:, 0, :], a_log.to_broadcast([P, HEADS])).then_inc(S["par_in"], 16)
            sp.dma_start(decay_par[:, 1, :], dt_bias.to_broadcast([P, HEADS])).then_inc(S["par_in"], 16)
            sp.wait_ge(S["iota_done"], 1)
            sp.dma_start(rows[0:2 * FT, 0:3, :], ffn_conv_w[0].rearrange("a (r n) -> r a n", n=P))\
              .then_inc(S["rows_in"], 16)
            sp.dma_start(rows[0:2 * FT, 3, :], ffn_conv_b.rearrange("a (r n) -> (a r) n", n=P))\
              .then_inc(S["rows_in"], 16)
            sp.dma_start(rows[0:3 * HEADS, 4:8, :], conv_qkv_w[0].rearrange("a (r n) -> r a n", n=P))\
              .then_inc(S["rows_in"], 16)
            sp.dma_start(rows[0:PG, 8, :], pool_b[0]).then_inc(S["rows_in"], 16)
            sp.dma_start(rows[0:PG, 9, :], pool_scale.rearrange("a (r n) -> (a r) n", n=P))\
              .then_inc(S["rows_in"], 16)
            sp.dma_start(rows[0:1, 10, :], onorm_w).then_inc(S["rows_in"], 16)
            sp.dma_start(pool_wt[:, :, :], pool_w[0].rearrange("g c d -> c g d"))\
              .then_inc(S["pool_w_in"], 16)
            sp.wait_ge(S["normed_done"], TT)
            sp.dma_start(norm_row[:, :], norm2_w.to_broadcast([P, D])).then_inc(S["norm_row_in"], 16)
            for n in range(2, N_IN):
                slab(n)
            for n, k in enumerate(K_ORDER):
                if n < 2:
                    sp.wait_ge(S["slab_lo"], N_IN - 1 + n)
                else:
                    sp.wait_ge(S["wo_lo"], n - 1)
                sp.dma_start(stage[:, n % 2, :], w_out_k[k]).then_inc(stage_in[n % 2], 16)
            for t in range(TT):
                sp.wait_ge(S["ot_lo"], tile_split(t))
                sp.dma_start(res[:, t, :], x_t[t]).then_inc(x_in[t], 16)
                if t == 0:
                    sp.wait_ge(S["wo_lo"], KT)
                    load_up(sp, 0, 0, 0)
                    load_up(sp, 0, 0, 1)
            sp.wait_ge(S["normed_done"], 2 * TT)
            sp.dma_start(norm_row[:, :], final_norm_w.unsqueeze(0).to_broadcast([P, D]))\
              .then_inc(S["norm_row_in"], 16)
            sp.wait_ge(S["ffn_lo"], 1)
            load_up(sp, 0, 1, 0)
            sp.wait_ge(S["ffn_lo"], 2)
            load_up(sp, 0, 1, 1)
            with sp.Fori(0, (FG - 1) // 2) as m:
                for b in range(2):
                    for n in range(6):
                        sp.wait_ge(S["ffn_lo"], m * 12 + (6 * b + n + 3))
                        if n < 4:
                            load_up(sp, m * 2 + (1 + b), n // 2, n % 2)
                        else:
                            load_down(sp, m * 4 + (2 * b + n - 4), n % 2)
            for e in range(2):
                sp.wait_ge(S["ffn_lo"], 4 + 6 * (FG - 1) + e - 1)
                load_down(sp, FT - 2 + e, e)
            for t in range(TT):
                sp.wait_ge(S["final_done"], t + 1)
                sp.dma_start(out_t[t], res[:, t, :]).then_inc(S["out_written"], 16)
            sp.wait_ge(S["out_written"], 16 * TT)

        STAGED = 16 * (N_IN + KT) // 2

        @block.gpsimd
        def _(pool_):
            pool_.memset(rows[:, :, :], 0.0).then_inc(S["iota_done"], 1)
            pool_.iota(col_i[:, :], pattern=[[1, CHUNK]], base=0, channel_multiplier=0)\
                .then_inc(S["iota_done"], 1)
            for par in range(2):
                pool_.wait_ge(S["iota_done"], 2 + par)
                pool_.iota(row_i[rows_of(par), :], pattern=[[0, CHUNK]], base=0,
                           channel_multiplier=1).then_inc(S["iota_done"], 1)
            pool_.wait_ge(S["iota_done"], 4)
            pool_.memset(ident[:, :], 0.0).then_inc(S["ident_done"], 1)
            pool_.wait_ge(S["ident_done"], 1)
            pool_.affine_select(out=ident[:, :], in_=ident[:, :], compare_op=ALU.not_equal, fill=1.0,
                                base=0, pattern=[[-1, P]], channel_multiplier=1)\
                .then_inc(S["ident_done"], 1)

            def slab_lo(n):
                pool_.wait_ge(S["slab_hi"], n + 1)
                pool_.tensor_tensor(ring_lo[n % 2], stage[:, n % 2, :], ring_hi[n % 2].bitcast(F32),
                                    ALU.subtract).then_inc(S["slab_lo"], 1)

            def right_sides(h):
                pool_.wait_ge(S["ex_done"], 1)
                if h:
                    pool_.wait_ge(S["xt_upd"], 6 * h)
                pool_.tensor_tensor(b3(r1), bc(g_tok[:, h, :], CHUNK), bm(m_gt[:, :]), ALU.mult)\
                    .then_inc(S["rhs_done"], 1)
                pool_.tensor_tensor(b3(r2), bc(g_tok[:, h, :], CHUNK), bm(m_le[:, :]), ALU.mult)\
                    .then_inc(S["rhs_done"], 1)
                pool_.tensor_tensor(b3(r3), bc(beta[:, h, :], CHUNK), bm(m_eq[:, :]), ALU.mult)\
                    .then_inc(S["rhs_done"], 1)

            for n in range(4):
                slab_lo(n)
            pool_.memset(aqkT[:, :, :, :], 0.0).then_inc(S["aqk_cleared"], 1)
            pool_.wait_ge(S["consts_done"], 8)
            for h in range(HEADS):
                slab_lo(4 * h + 4)
                right_sides(h)
                slab_lo(4 * h + 5)
                pool_.wait_ge(S["gam_done"], h + 1)
                if h:
                    pool_.wait_ge(S["aqk_done"], 2 * h)
                pool_.tensor_tensor(b3(gti), b3(gam[:, 1, :]), bm(m_le[:, :]), ALU.mult)\
                    .then_inc(S["gti_done"], 1)
                pool_.tensor_tensor(b3(gam[:, 0, :]), b3(gam[:, 0, :]), bm(m_pair[:, :]), ALU.mult)\
                    .then_inc(S["g1_done"], 1)
                pool_.wait_ge(S["g1_done"], 2 * h + 1)
                pool_.tensor_tensor(b3(gam[:, 0, :]), b3(gam[:, 0, :]), bc(beta[:, h, :], CHUNK),
                                    ALU.mult).then_inc(S["g1_done"], 1)
                for lv in range(LEVELS):
                    pool_.wait_ge(S["lt_done"], h + 1)
                    if lv >= 2:
                        pool_.wait_ge(S["t1_mm"], LEVELS * h + lv - 1)
                    else:
                        pool_.wait_ge(S["beta_mm"], h + 1)
                    pool_.tensor_tensor(b3(bt[lv % 2]), b3(ltT), bm(m_level[:, lv + 1, :]), ALU.mult)\
                        .then_inc(S["bt_done"], 1)
                    if lv == 1:
                        slab_lo(4 * h + 6)
                slab_lo(4 * h + 7)

            def ffn_lo(n, slot, ring):
                pool_.wait_ge(S["ffn_hi"], n)
                pool_.tensor_tensor(ring_lo[ring], stage[:, slot, :], ring_hi[ring].bitcast(F32),
                                    ALU.subtract).then_inc(S["ffn_lo"], 1)

            def act_lo_of(n, e, slot):
                pool_.wait_ge(S["act_hi_done"], n)
                pool_.tensor_tensor(act_lo[:, slot, :], up_conv[:, e, 0, :],
                                    act_hi[:, slot, :].bitcast(F32), ALU.subtract)\
                    .then_inc(S["act_lo_done"], 1)

            for n in range(5):
                ffn_lo(n + 1, n % 2, n % 3)
            act_lo_of(1, 0, 0)
            with pool_.Fori(0, (FG - 1) // 2) as m:
                for b in range(2):
                    par = (1 + b) % 2
                    for n in range(1, 7):
                        if n == 4:
                            act_lo_of(m * 4 + (2 * b + 2), 1, 2 * (1 - par) + 1)
                        if n == 5:
                            act_lo_of(m * 4 + (2 * b + 3), 0, 2 * par)
                        ffn_lo(m * 12 + (4 + 6 * b + n + 1), n % 2, (1 + n) % 3)
            last = 4 + 6 * (FG - 1)
            ffn_lo(last + 2, 1, SPARE)
            act_lo_of(2 * FG, 1, 2 * ((FG - 1) % 2) + 1)

        @block.scalar
        def _(act):
            act.dma_start(norm_row[:, :], norm1_w.to_broadcast([P, D])).then_inc(S["norm_row_in"], 16)
            act.dma_start(wba[:, :, :], w_in_k[:, :, 4 * DN:4 * DN + 2 * HEADS])\
                .then_inc(S["ba_w_in"], 16)
            act.preload_act_table_set(LN_EXP_SET)

            def rstd(n, t):
                squares = k_be
                if n >= TT:
                    act.wait_ge(S["normed_T"], n - 1)
                    squares = normed[:, n % 2, :]
                act.activation(squares, res[:, t, :], ACT.Square,
                               accum_out=stats[:, 0, t:t + 1]).then_inc(S["sq_done"], 1)
                act.wait_ge(S["sq_done"], n + 1)
                act.activation(stats[:, 1, t:t + 1], stats[:, 0, t:t + 1], ACT.Ln,
                               scale=1.0 / D, bias=eps_b[:, :]).then_inc(S["ln_done"], 1)
                act.wait_ge(S["ln_done"], n + 1)
                act.activation(stats[:, 2, t:t + 1], stats[:, 1, t:t + 1], ACT.Exp, scale=-0.5)\
                    .then_inc(S["rstd_done"], 1)

            def h_hi(n, t, dst, b):
                act.wait_ge(S["normed_T"], n + 1)
                act.activation(dst[:, :, t * P:(t + 1) * P], b3(bank(b, 2), P), ACT.Copy)\
                    .then_inc(S["h_hi"], 1)

            def slab_hi(n):
                act.wait_ge(stage_in[n % 2], 16 * (n // 2 + 1))
                if n >= 2:
                    act.wait_ge(S["dense_done"], slab_used(n - 2))
                act.activation(ring_hi[n % 2], stage[:, n % 2, :], ACT.Copy).then_inc(S["slab_hi"], 1)

            evacuated = [0]

            def evacuate_to(n):
                while evacuated[0] < n:
                    g = evacuated[0]
                    kind, i, j, half = GROUPS[g]
                    act.wait_ge(S["dense_done"], g + 1)
                    src = bank(g % 2)
                    gp = PG - 1 - j
                    to_cat = cat[:, 4 * half:4 * half + 4, i if kind == "proj" else HEADS + gp, :]
                    if kind == "lin":
                        act.wait_ge(S["cols_done"], 2)
                        act.activation(to_cat, b3(src, P), ACT.Identity, scale=cols[:, 9, gp:gp + 1],
                                       bias=pool_bias[:, gp:gp + 1]).then_inc(S["dense_evac"], 1)
                    elif i < HEADS and j == 3:
                        act.activation(to_cat, b3(src, P), ACT.Silu).then_inc(S["dense_evac"], 1)
                        if half == 0:
                            silu(i, 0)
                            silu(i, 1)
                            squares(i)
                        else:
                            silu(i, 2)
                    else:
                        if i < HEADS:
                            if i:
                                act.wait_ge(S["conv_step"], 12 * (i - 1) + 4 * (j + 1))
                            dst = raw[:, j, half * HALF:(half + 1) * HALF]
                        else:
                            act.wait_ge(S["conv_step"], 12 * HEADS)
                            if j >= 2:
                                act.wait_ge(S["dense_done"], INDEX[("lin", HEADS, j - 2, 1)] + 1)
                            dst = raw[:, j % 2, half * HALF:(half + 1) * HALF]
                        act.activation(dst, src, ACT.Copy).then_inc(S["dense_evac"], 1)
                    evacuated[0] += 1
                    if kind == "proj" and half == 1 and 4 * i + j + 2 < N_IN:
                        slab_hi(4 * i + j + 2)

            def silu(i, j):
                act.wait_ge(S["conv_step"], 12 * i + 4 * (j + 1))
                act.activation(qkv[:, j, :], qkv[:, j, :], ACT.Silu).then_inc(S["silu_done"], 1)

            def squares(i):
                if i:
                    act.wait_ge(S["w_mm"], i)
                act.wait_ge(S["silu_done"], 3 * i + 1)
                act.activation(k_be, qkv[:, 0, :], ACT.Square).then_inc(S["sumsq_in"], 1)
                act.wait_ge(S["silu_done"], 3 * i + 2)
                act.activation(gam_flat, qkv[:, 1, :], ACT.Square).then_inc(S["sumsq_in"], 1)

            act.wait_ge(S["eps_done"], 2)
            act.wait_ge(x_in[0], 16)
            rstd(0, 0)
            for t in range(TT):
                if t + 1 < TT:
                    act.wait_ge(x_in[t + 1], 16)
                    rstd(t + 1, t + 1)
                if t:
                    h_hi(t - 1, t - 1, a_hi, 2 + 2 * ((t - 1) % 2))
                if t == 7:
                    evacuate_to(1)
            h_hi(TT - 1, TT - 1, a_hi, 2 + 2 * ((TT - 1) % 2))
            evacuate_to(2)
            act.wait_ge(S["cols_T"], 1)
            act.activation(cols[:, :, :].rearrange("p a b -> p (a b)"), bank(6)[:, 0:484], ACT.Copy)\
                .then_inc(S["cols_done"], 1)
            evacuate_to(3)
            act.wait_ge(S["ba_done"], 1)
            act.activation(sc[:, 0, :, :], ba[:, 0:HEADS, :], ACT.Exp, scale=-1.0)\
                .then_inc(S["sc_act"], 1)
            act.wait_ge(S["par_in"], 32)
            act.activation(decay_par[:, 2, :], decay_par[:, 0, :], ACT.Exp).then_inc(S["sc_act"], 1)
            act.wait_ge(S["sc_dve"], 3)
            act.activation(sc[:, 2, :, :], sc[:, 2, :, :], ACT.Exp).then_inc(S["sc_act"], 1)
            act.wait_ge(S["sc_dve"], 4)
            act.activation(sc[:, 3, :, :], sc[:, 4, :, :], ACT.Ln).then_inc(S["sc_act"], 1)
            act.wait_ge(S["cum_mm"], 1)
            act.activation(ex[:, :, :, :].rearrange("p a h b -> p (a h b)"),
                           bank(6)[:, 0:4 * HEADS * TT], ACT.Exp).then_inc(S["ex_done"], 1)

            def square_o(h):
                act.wait_ge(S["o_evac"], 2 * (h + 1))
                act.wait_ge(S["v_new_done"], NCH * (h + 1))
                act.activation(v_tok, o_T, ACT.Square).then_inc(S["sqo_done"], 1)

            def norm_o(h):
                act.wait_ge(S["sumsq_o_mm"], h + 1)
                act.activation(v_tok, bank(6, 2), ACT.Ln, scale=1.0 / P, bias=eps_b[:, :])\
                    .then_inc(S["ln_o"], 1)
                act.wait_ge(S["ln_o"], h + 1)
                act.activation(v_tok, v_tok, ACT.Exp, scale=-0.5).then_inc(S["r_o"], 1)

            for i in range(HEADS + 1):
                h = i - 1
                if h >= 0:
                    for s, (step, _) in enumerate(STEPS):
                        if s >= 2:
                            evacuate_to(groups_done(i, s))
                        if step == "start":
                            act.preload_act_table_set(LN_EXP_SET)
                        elif step == "sumsq_q":
                            if h:
                                square_o(h - 1)
                            act.wait_ge(S["sumsq_q_mm"], h + 1)
                            act.activation(k_be, bank(4, 2), ACT.Ln, bias=eps_b[:, :])\
                                .then_inc(S["lnq"], 1)
                            act.wait_ge(S["lnq"], h + 1)
                            act.activation(k_be, k_be, ACT.Exp, scale=-0.5, bias=bias_q[:, :])\
                                .then_inc(S["rq"], 1)
                        elif step == "norm_o":
                            if h:
                                norm_o(h - 1)
                        elif step == "sumsq_k":
                            act.wait_ge(S["sumsq_k_mm"], h + 1)
                            if h:
                                act.wait_ge(S["o_mm"], 2 * h)
                            act.activation(k_d, bank(2, 2), ACT.Ln, bias=eps_b[:, :])\
                                .then_inc(S["lnk"], 1)
                            act.wait_ge(S["lnk"], h + 1)
                            act.activation(k_d, k_d, ACT.Exp, scale=-0.5).then_inc(S["rk"], 1)
                        elif step == "decay":
                            act.wait_ge(S["decay_mm"], h + 1)
                            if h:
                                act.wait_ge(S["l1_done"], h)
                            act.activation(gam[:, :, :].rearrange("p a n -> p (a n)"), bank(4, 2), ACT.Exp)\
                                .then_inc(S["gam_done"], 1)
                        elif step == "decay_row":
                            act.wait_ge(S["decay_row_mm"], h + 1)
                            if h:
                                act.wait_ge(S["on_done"], h)
                                act.wait_ge(S["head_done"], h)
                            act.activation(o_T, bank(2, 2), ACT.Exp).then_inc(S["erow_done"], 1)
                        elif step.startswith("level") and step.endswith("a"):
                            lv = int(step[5])
                            act.wait_ge(S["t1_mm"], LEVELS * h + lv + 1)
                            act.activation(t1, bank(2), ACT.Copy).then_inc(S["t1_evac"], 1)
                        elif step == "u":
                            act.wait_ge(S["u_mm"], h + 1)
                            act.activation(v_tok, bank(2, 2), ACT.Copy).then_inc(S["u_evac"], 1)
                        elif step == "w":
                            act.wait_ge(S["w_mm"], h + 1)
                            act.activation(wT, bank(4, 2), ACT.Copy).then_inc(S["w_evac"], 1)
                        elif step.startswith("chunk") and step.endswith("b"):
                            c = int(step[5:-1])
                            if c % 8 == 7:
                                q = c // 8
                                act.wait_ge(S["o_mm"], 2 * h + q + 1)
                                act.wait_ge(S["qg_done"], h + 1)
                                act.activation(o_T[:, q * HALF:(q + 1) * HALF], bank(o_bank(c)), ACT.Copy)\
                                    .then_inc(S["o_evac"], 1)
                if i < HEADS:
                    evacuate_to(PASS_START[i + 1])
            def wo_hi(n):
                act.wait_ge(stage_in[n % 2], 16 * (N_IN // 2 + n // 2 + 1))
                act.activation(a_hi[:, K_ORDER[n], :], stage[:, n % 2, :], ACT.Copy)\
                    .then_inc(S["wo_hi"], 1)

            def split_part(part):
                lo, hi = (k * P for k in CAT_PARTS[part])
                for t in range(2):
                    act.activation(ring_hi[t][:, lo:hi], res[:, t, lo:hi], ACT.Copy)\
                        .then_inc(S["ot_hi"], 1)

            def split_cat(t):
                act.wait_ge(S["res_mm"], 2 * (t - 1))
                act.activation(ring_hi[t % 2], res[:, t, :], ACT.Copy).then_inc(S["ot_hi"], 1)

            square_o(HEADS - 1)
            evacuate_to(INDEX[("proj", HEADS, 3, 1)] + 1)
            wo_hi(0)
            act.wait_ge(S["head_done"], HEADS - 1)
            split_part(0)
            wo_hi(1)
            evacuate_to(INDEX[("lin", HEADS, 2, 1)] + 1)
            norm_o(HEADS - 1)
            wo_hi(2)
            evacuate_to(NG)
            wo_hi(3)
            act.wait_ge(S["dense_evac"], NG)
            split_part(1)
            wo_hi(4)
            act.wait_ge(S["head_done"], HEADS)
            split_part(2)
            for n in range(5, KT):
                wo_hi(n)

            def ffn_hi(arrivals, slot, ring, free, free_at):
                act.wait_ge(stage_in[slot], arrivals)
                act.wait_ge(free, free_at)
                act.activation(ring_hi[ring], stage[:, slot, :], ACT.Copy).then_inc(S["ffn_hi"], 1)

            def evacuate_up(n, e, gu, half, conv_at):
                act.wait_ge(S["up_mm"], n)
                if conv_at is not None:
                    act.wait_ge(S["up_conv_step"], conv_at)
                act.activation(up_raw[:, e, gu, half * HALF:(half + 1) * HALF],
                               bank(2 * gu + half), ACT.Copy).then_inc(S["raw_evac"], 1)

            def gate_silu(e, steps):
                act.wait_ge(S["up_conv_step"], steps)
                act.activation(up_conv[:, e, 0, :], up_conv[:, e, 0, :], ACT.Silu)\
                    .then_inc(S["gate_silu"], 1)

            def split_act(e, acts, slot, down_at):
                act.wait_ge(S["act_done"], acts)
                if down_at is not None:
                    act.wait_ge(S["res_mm"], down_at)
                act.activation(act_hi[:, slot, :], up_conv[:, e, 0, :], ACT.Copy)\
                    .then_inc(S["act_hi_done"], 1)

            for t in range(TT):
                if t + 2 < TT:
                    split_cat(t + 2)
                if t == TT - 1:
                    ffn_hi(STAGED + 16, 0, 0, S["res_mm"], 2 * TT - 2)
                    ffn_hi(STAGED + 16, 1, 1, S["res_mm"], 2 * TT)
                act.wait_ge(S["res_add"], 2 * (t + 1))
                rstd(TT + t, t)
                if t:
                    h_hi(TT + t - 1, t - 1, h2_hi, h2_bank(t - 1))
            act.preload_act_table(ACT.Silu)
            evacuate_up(1, 0, 0, 0, None)
            h_hi(2 * TT - 1, TT - 1, h2_hi, h2_bank(TT - 1))
            ffn_hi(STAGED + 32, 0, 2, S["normed_T"], 2 * TT)
            evacuate_up(2, 0, 1, 0, None)
            evacuate_up(3, 0, 0, 1, None)
            ffn_hi(STAGED + 32, 1, 0, S["up_mm"], 3)
            evacuate_up(4, 0, 1, 1, None)
            evacuate_up(5, 1, 0, 0, None)
            ffn_hi(STAGED + 48, 0, 1, S["up_mm"], 4)
            gate_silu(0, 3)
            evacuate_up(6, 1, 0, 1, None)
            split_act(0, 1, 0, None)
            evacuate_up(7, 1, 1, 0, None)
            gate_silu(1, 9)
            evacuate_up(8, 1, 1, 1, None)
            with act.Fori(0, (FG - 1) // 2) as m:
                for b in range(2):
                    par = (1 + b) % 2

                    def at(n):
                        return m * 16 + (8 * (1 + b) + n)

                    def staged(n):
                        return m * (16 * 6) + (STAGED + 16 * ((4 + 6 * b + n) // 2 + 1))

                    def ups(n):
                        e, gu, half = n // 4, (n // 2) % 2, n % 2
                        evacuate_up(at(n + 1), e, gu, half, m * 24 + (12 * b + 6 * e + 3 * gu + 3))

                    ffn_hi(staged(1), 1, 2, S["res_mm"], m * 32 + 16 * (b + 1))
                    ups(0)
                    ffn_hi(staged(2), 0, 0, S["res_mm"], m * 32 + 16 * (b + 1))
                    ups(1)
                    ffn_hi(staged(3), 1, 1, S["up_mm"], at(2))
                    split_act(1, m * 4 + (2 * b + 2), 2 * (1 - par) + 1, None)
                    ups(2)
                    ups(3)
                    ffn_hi(staged(4), 0, 2, S["up_mm"], at(4))
                    gate_silu(0, m * 24 + (12 * b + 15))
                    ups(4)
                    split_act(0, m * 4 + (2 * b + 3), 2 * par, m * 32 + 16 * (b + 1))
                    ups(5)
                    ffn_hi(staged(5), 1, 0, S["up_mm"], at(6))
                    ups(6)
                    gate_silu(1, m * 24 + (12 * b + 21))
                    ups(7)
                    ffn_hi(staged(6), 0, 1, S["up_mm"], at(8))
            last = 4 + 6 * (FG - 1)
            ffn_hi(STAGED + 16 * (last // 2 + 1), 1, SPARE, S["up_conv_step"], 12 * (FG - 1) + 6)
            split_act(1, 2 * FG, 2 * ((FG - 1) % 2) + 1, None)
            act.preload_act_table_set(LN_EXP_SET)
            for t in range(TT):
                act.wait_ge(S["res_add"], 2 * TT * FG + 2 * (t + 1))
                act.activation(up_conv[:, 0, 0, :], res[:, t, :], ACT.Square,
                               accum_out=stats[:, 0, t:t + 1]).then_inc(S["final_sq"], 1)
                act.wait_ge(S["final_sq"], t + 1)
                act.activation(stats[:, 1, t:t + 1], stats[:, 0, t:t + 1], ACT.Ln,
                               scale=1.0 / D, bias=eps_b[:, :]).then_inc(S["final_ln"], 1)
                act.wait_ge(S["final_ln"], t + 1)
                act.activation(stats[:, 2, t:t + 1], stats[:, 1, t:t + 1], ACT.Exp, scale=-0.5)\
                    .then_inc(S["final_r"], 1)

        @block.vector
        def _(dve):
            dve.memset(eps_b[:, :], EPS).then_inc(S["eps_done"], 1)
            dve.memset(bias_q[:, :], -0.5 * float(np.log(P))).then_inc(S["eps_done"], 1)
            def first_slab_hi(n):
                dve.wait_ge(stage_in[n], 16)
                dve.tensor_copy(ring_hi[n], stage[:, n, :]).then_inc(S["slab_hi"], 1)

            def norm(n, t):
                dve.wait_ge(S["rstd_done"], n + 1)
                if n >= 2:
                    dve.wait_ge(S["normed_T"], n - 1)
                dve.scalar_tensor_tensor(normed[:, n % 2, :], res[:, t, :], stats[:, 2, t:t + 1],
                                         norm_row[:, :], ALU.mult, ALU.mult)\
                   .then_inc(S["normed_done"], 1)

            def h_lo(n, t, hi, lo, b):
                dve.wait_ge(S["h_hi"], n + 1)
                c = slice(t * P, (t + 1) * P)
                dve.tensor_tensor(lo[:, :, c], b3(bank(b, 2), P), hi[:, :, c].bitcast(F32), ALU.subtract)\
                   .then_inc(S["h_lo"], 1)

            dve.wait_ge(S["norm_row_in"], 16)
            norm(0, 0)
            norm(1, 1)
            for t in range(1, TT + 1):
                if t + 1 < TT:
                    norm(t + 1, t + 1)
                h_lo(t - 1, t - 1, a_hi, a_lo, 2 + 2 * ((t - 1) % 2))
                if t in (2, 3):
                    first_slab_hi(t - 2)
                if t == 1:
                    dve.wait_ge(S["ba_w_in"], 16)
                    dve.tensor_copy(wba_hi[:, :, :], wba[:, :, :]).then_inc(S["ba_w_split"], 1)
                    dve.wait_ge(S["ba_w_split"], 1)
                    dve.tensor_tensor(wba_lo[:, :, :], wba[:, :, :], wba_hi[:, :, :].bitcast(F32), ALU.subtract)\
                       .then_inc(S["ba_w_split"], 1)
                if t == 6:
                    dve.wait_ge(S["ba_mm"], 1)
                    dve.tensor_copy(ba_T[:, 0:HALF], bank(6)[0:8, :]).then_inc(S["ba_evac"], 1)
            dve.wait_ge(S["iota_done"], 4)
            dve.tensor_tensor(m_le[:, :], row_i[:, :], col_i[:, :], ALU.is_le).then_inc(S["cmp_done"], 1)
            dve.tensor_tensor(m_gt[:, :], row_i[:, :], col_i[:, :], ALU.is_gt).then_inc(S["cmp_done"], 1)
            dve.tensor_tensor(m_lt[:, :], row_i[:, :], col_i[:, :], ALU.is_lt).then_inc(S["cmp_done"], 1)
            dve.tensor_tensor(m_eq[:, :], row_i[:, :], col_i[:, :], ALU.is_equal)\
               .then_inc(S["cmp_done"], 1)
            dve.tensor_tensor(xor_i[:, :], row_i[:, :], col_i[:, :], ALU.bitwise_xor)\
               .then_inc(S["cmp_done"], 1)
            dve.tensor_scalar(inv_pos[:, :], col_i[:, 0:16], 1.0, None, ALU.add)\
               .then_inc(S["cmp_done"], 1)
            for m in (tri, suf, blk_ones, half_ones):
                dve.memset(m[:], 0.0).then_inc(S["mask_done"], 1)
            dve.memset(ones[:, :], 1.0).then_inc(S["mask_done"], 1)
            dve.wait_ge(S["cmp_done"], 6)
            for k in range(6):
                dve.tensor_scalar(shift_i[:, k, :], xor_i[:, :], k, None, ALU.logical_shift_right)\
                   .then_inc(S["cmp_done"], 1)
            dve.reciprocal(inv_pos[:, :], inv_pos[:, :]).then_inc(S["cmp_done"], 1)
            dve.wait_ge(S["cmp_done"], 13)
            for k in range(6):
                dve.scalar_tensor_tensor(m_level[:, k, :], shift_i[:, k, :], 1.0, m_lt[:, :],
                                         ALU.is_equal, ALU.mult).then_inc(S["mask_done"], 1)
            dve.scalar_tensor_tensor(m_pair[:, :], shift_i[:, 0, :], 1.0, m_gt[:, :],
                                     ALU.is_equal, ALU.mult).then_inc(S["mask_done"], 1)
            dve.wait_ge(S["mask_done"], 12)
            for par in range(2):
                r = rows_of(par)
                dve.tensor_copy(tri[r, r], m_le[r, :]).then_inc(S["consts_done"], 1)
                dve.tensor_copy(suf[r, r], m_gt[r, :]).then_inc(S["consts_done"], 1)
                dve.memset(blk_ones[r, r], 1.0).then_inc(S["consts_done"], 1)
                dve.memset(half_ones[r, par, :], 1.0).then_inc(S["consts_done"], 1)
            dve.wait_ge(S["ba_mm"], 2)
            dve.tensor_copy(ba_T[:, HALF:SEQ], bank(7)[0:8, :]).then_inc(S["ba_evac"], 1)
            dve.wait_ge(S["ba_T_mm"], 1)
            dve.tensor_copy(ba[:, :, :], bank(7)[:, 0:8 * TT].rearrange("p (b c) -> p c b", c=8))\
               .then_inc(S["ba_done"], 1)
            dve.wait_ge(S["ba_done"], 1)
            dve.wait_ge(S["par_in"], 32)
            dve.tensor_tensor(sc[:, 1, :, :], ba[:, HEADS:2 * HEADS, :],
                              decay_par[:, 1, :].unsqueeze(2).to_broadcast([P, HEADS, TT]), ALU.add)\
               .then_inc(S["sc_dve"], 1)
            dve.wait_ge(S["sc_dve"], 1)
            dve.tensor_scalar(sc[:, 2, :, :], sc[:, 1, :, :], -1.0, None, ALU.mult)\
               .then_inc(S["sc_dve"], 1)
            dve.wait_ge(S["sc_dve"], 2)
            dve.tensor_tensor(sc[:, 2, :, :], sc[:, 1, :, :], sc[:, 2, :, :], ALU.min)\
               .then_inc(S["sc_dve"], 1)
            dve.wait_ge(S["sc_act"], 3)
            dve.tensor_scalar(sc[:, 4, :, :], sc[:, 2, :, :], 1.0, None, ALU.add)\
               .then_inc(S["sc_dve"], 1)
            dve.tensor_scalar(sc[:, 0, :, :], sc[:, 0, :, :], 1.0, None, ALU.add)\
               .then_inc(S["sc_dve"], 1)
            dve.wait_ge(S["sc_dve"], 5)
            dve.reciprocal(beta[:, :, :], sc[:, 0, :, :]).then_inc(S["sc_dve"], 1)
            dve.tensor_scalar(sc[:, 5, :, :], sc[:, 4, :, :], -1.0, None, ALU.add)\
               .then_inc(S["sc_dve"], 1)
            dve.wait_ge(S["sc_dve"], 7)
            dve.tensor_tensor(sc[:, 5, :, :], sc[:, 2, :, :], sc[:, 5, :, :], ALU.subtract)\
               .then_inc(S["sc_dve"], 1)
            dve.reciprocal(sc[:, 0, :, :], sc[:, 4, :, :]).then_inc(S["sc_dve"], 1)
            dve.tensor_scalar(sc[:, 1, :, :], sc[:, 1, :, :], 0.0, None, ALU.max)\
               .then_inc(S["sc_dve"], 1)
            dve.wait_ge(S["sc_dve"], 10)
            dve.tensor_tensor(sc[:, 5, :, :], sc[:, 5, :, :], sc[:, 0, :, :], ALU.mult)\
               .then_inc(S["sc_dve"], 1)
            dve.wait_ge(S["sc_dve"], 11)
            dve.tensor_tensor(sc[:, 1, :, :], sc[:, 1, :, :], sc[:, 5, :, :], ALU.add)\
               .then_inc(S["sc_dve"], 1)
            dve.wait_ge(S["sc_dve"], 12)
            dve.wait_ge(S["sc_act"], 4)
            dve.tensor_tensor(sc[:, 1, :, :], sc[:, 1, :, :], sc[:, 3, :, :], ALU.add)\
               .then_inc(S["sc_dve"], 1)
            dve.wait_ge(S["sc_dve"], 13)
            dve.scalar_tensor_tensor(g_tok[:, :, :], sc[:, 1, :, :], -1.0,
                                     decay_par[:, 2, :].unsqueeze(2).to_broadcast([P, HEADS, TT]),
                                     ALU.mult, ALU.mult).then_inc(S["sc_dve"], 1)
            dve.wait_ge(S["ex_done"], 1)
            dve.tensor_tensor(beg[:, :, :], beta[:, :, :], ex[:, 0, :, :], ALU.mult)\
               .then_inc(S["sc_dve"], 1)
            dve.wait_ge(S["sc_dve"], 15)
            dve.wait_ge(S["cols_done"], 1)
            dve.tensor_tensor(pool_bias[:, :], cols[:, 8, 0:PG], cols[:, 9, 0:PG], ALU.mult)\
               .then_inc(S["cols_done"], 1)

            conv_at = [0]

            def conv_op(i, seen):
                j, tap = divmod(conv_at[0] - 12 * i, 4)
                if j >= 3 or INDEX[("proj", i, j, 1)] >= seen:
                    return
                w = cols[:, 4 + (3 - tap), j * HEADS + i:j * HEADS + i + 1]
                if tap == 0:
                    dve.wait_ge(S["dense_evac"], INDEX[("proj", i, j, 1)] + 1)
                    dve.tensor_scalar(qkv[:, j, :], raw[:, j, :], w, None, ALU.mult)\
                       .then_inc(S["conv_step"], 1)
                else:
                    dve.wait_ge(S["conv_step"], conv_at[0])
                    dve.scalar_tensor_tensor(qkv[:, j, tap:SEQ], raw[:, j, 0:SEQ - tap], w,
                                             qkv[:, j, tap:SEQ], ALU.mult, ALU.add)\
                       .then_inc(S["conv_step"], 1)
                conv_at[0] += 1

            pool_at = [0, 0, 0]

            def pool_op(seen):
                j, n, done = pool_at
                if j >= PG or INDEX[("proj", HEADS, j, 1)] >= seen:
                    return
                u = raw[:, j % 2, :]
                src = u if n == 0 else (raw[:, 2, :], gam_flat)[(n - 1) % 2]
                dst = (raw[:, 2, :], gam_flat)[n % 2]
                lag = 1 << n
                if n == 0:
                    dve.wait_ge(S["dense_evac"], INDEX[("proj", HEADS, j, 1)] + 1)
                if done:
                    dve.wait_ge(S["pooled_step"], done)
                if n <= PG - 1 - j:
                    dve.tensor_copy(dst[:, 0:lag], src[:, 0:lag]).then_inc(S["pooled_step"], 1)
                    dve.tensor_tensor(dst[:, lag:SEQ], src[:, lag:SEQ], src[:, 0:SEQ - lag], ALU.add)\
                       .then_inc(S["pooled_step"], 1)
                    pool_at[:] = [j, n + 1, done + 2]
                else:
                    w = POOL_WINDOWS[PG - 1 - j]
                    dve.scalar_tensor_tensor(src[:, 0:w - 1], src[:, 0:w - 1], float(w),
                                             inv_pos[:, 0:w - 1], ALU.mult, ALU.mult)\
                       .then_inc(S["pooled_step"], 1)
                    dve.wait_ge(S["pooled_step"], done + 1)
                    dve.scalar_tensor_tensor(u, src, 1.0 / w, u, ALU.mult, ALU.subtract)\
                       .then_inc(S["pooled_step"], 1)
                    pool_at[:] = [j + 1, 0, done + 2]

            def fill(i, seen):
                if i < HEADS:
                    conv_op(i, seen)
                else:
                    pool_op(seen)

            def norm_o(h):
                dve.wait_ge(S["r_o"], h + 1)
                dve.tensor_tensor(o_T, o_T, v_tok, ALU.mult).then_inc(S["on_done"], 1)
                dve.wait_ge(S["on_done"], h + 1)
                dve.scalar_tensor_tensor(cat[:, :, h, :], b3(o_T, P), cols[:, 10, 0:1], cat[:, :, h, :],
                                         ALU.mult, ALU.mult).then_inc(S["head_done"], 1)

            for i in range(HEADS + 1):
                h = i - 1
                for s, (step, _) in enumerate(STEPS if h >= 0 else ()):
                    if step == "norm_o" and h:
                        norm_o(h - 1)
                    elif step == "vT":
                        dve.wait_ge(S["v_T_mm"], h + 1)
                        if h:
                            dve.wait_ge(S["on_done"], h)
                        dve.tensor_tensor(b3(v_tok, P), b3(bank(6, 2), P), bc(beta[:, h, :], P), ALU.mult)\
                           .then_inc(S["vb_done"], 1)
                    elif step == "sumsq_q":
                        dve.wait_ge(S["rq"], h + 1)
                        dve.tensor_tensor(qkv[:, 0, :], qkv[:, 0, :], k_be, ALU.mult)\
                           .then_inc(S["qn_done"], 1)
                    elif step == "sumsq_k":
                        dve.wait_ge(S["rk"], h + 1)
                        dve.tensor_tensor(qkv[:, 1, :], qkv[:, 1, :], k_d, ALU.mult)\
                           .then_inc(S["kn_done"], 1)
                    elif step == "beta_kk":
                        dve.wait_ge(S["gti_done"], h + 1)
                        dve.wait_ge(S["beta_mm"], h + 1)
                        dve.tensor_tensor(gam[:, 1, :], gam[:, 1, :], bank(4), ALU.mult)\
                           .then_inc(S["gtb_done"], 1)
                        dve.wait_ge(S["gtb_done"], h + 1)
                        dve.wait_ge(S["kk_mm"], h + 1)
                        dve.tensor_tensor(ltT, bank(5), gam[:, 1, :], ALU.mult).then_inc(S["lt_done"], 1)
                        dve.wait_ge(S["g1_done"], 2 * h + 2)
                        dve.tensor_tensor(tmp, bank(5), gam[:, 0, :], ALU.mult)\
                           .then_inc(S["l1_done"], 1)
                        dve.wait_ge(S["l1_done"], h + 1)
                        dve.tensor_tensor(b3(xinv), bm(m_eq[:, :]), b3(tmp), ALU.subtract)\
                           .then_inc(S["x_upd"], 1)
                        dve.wait_ge(S["lt_done"], h + 1)
                        dve.wait_ge(S["x_upd"], LEVELS * h + 1)
                        dve.tensor_tensor(b3(tmp), b3(ltT), bm(m_level[:, 0, :]), ALU.mult)\
                           .then_inc(S["tmpt_done"], 1)
                        dve.wait_ge(S["tmpt_done"], h + 1)
                        dve.tensor_tensor(b3(xinvT), bm(m_eq[:, :]), b3(tmp), ALU.subtract)\
                           .then_inc(S["xt_upd"], 1)
                    elif step == "qk":
                        dve.wait_ge(S["qk_mm"], h + 1)
                        dve.wait_ge(S["aqk_cleared"], 1)
                        for par in range(2):
                            r = rows_of(par)
                            dve.tensor_tensor(aqkT[r, :, par, :], b3(bank(2))[r], b3(gti)[r], ALU.mult)\
                               .then_inc(S["aqk_done"], 1)
                    elif step == "kT":
                        dve.wait_ge(S["k_T_mm"], h + 1)
                        dve.tensor_tensor(b3(k_be, P), b3(bank(4, 2), P), bc(beg[:, h, :], P), ALU.mult)\
                           .then_inc(S["kbe_done"], 1)
                        dve.tensor_tensor(b3(k_d, P), b3(bank(4, 2), P), bc(ex[:, 1, h, :], P), ALU.mult)\
                           .then_inc(S["kd_done"], 1)
                        dve.wait_ge(S["erow_done"], h + 1)
                        dve.tensor_tensor(qg.rearrange("p (b a n) -> p b a n", a=2, n=CHUNK),
                                          qkv[:, 0, :].rearrange("p (b a n) -> p b a n", a=2, n=CHUNK),
                                          o_T.rearrange("p (a b n) -> p b a n", a=2, n=CHUNK), ALU.mult)\
                           .then_inc(S["qg_done"], 1)
                    elif step.startswith("level") and step.endswith("b"):
                        lv = int(step[5])
                        if lv < LEVELS - 1:
                            dve.wait_ge(S["x_mm"], (LEVELS - 1) * h + lv + 1)
                            dve.tensor_tensor(xinv, xinv, bank(3), ALU.subtract).then_inc(S["x_upd"], 1)
                        dve.wait_ge(S["xt_mm"], LEVELS * h + lv + 1)
                        dve.tensor_tensor(xinvT, xinvT, bank(4), ALU.subtract).then_inc(S["xt_upd"], 1)
                        fill(i, groups_done(i, s - 1))
                    elif step == "w":
                        if h:
                            dve.wait_ge(S["s_upd"], (NCH + 1) * h)
                        dve.memset(state, 0.0).then_inc(S["s_upd"], 1)
                        fill(i, groups_done(i, s - 1))
                    elif step.startswith("chunk"):
                        c = int(step[5:-1])
                        r, blk = rows_of(c % 2), c // 2
                        if step.endswith("a"):
                            dve.wait_ge(S["v_mm"], NCH * h + c + 1)
                            if c == 0:
                                dve.wait_ge(S["u_evac"], h + 1)
                            dve.tensor_tensor(v_new[r, :], v_tok[r, blk * P:(blk + 1) * P],
                                              bank(6)[r, 0:P], ALU.subtract).then_inc(S["v_new_done"], 1)
                        else:
                            dve.wait_ge(S["s_mm"], NCH * h + c + 1)
                            dve.wait_ge(S["s_upd"], (NCH + 1) * h + c + 1)
                            dve.scalar_tensor_tensor(state, state, ex[:, 2 + c % 2, h, blk:blk + 1],
                                                     bank(6)[:, P:2 * P], ALU.mult, ALU.add)\
                               .then_inc(S["s_upd"], 1)
                            if c % 2:
                                fill(i, groups_done(i, s - 1))
                if i < HEADS:
                    while conv_at[0] < 12 * (i + 1):
                        conv_op(i, NG)

            def ot_lo(t):
                dve.wait_ge(S["ot_hi"], tile_split(t))
                dve.tensor_tensor(ring_lo[t % 2], res[:, t, :], ring_hi[t % 2].bitcast(F32),
                                  ALU.subtract).then_inc(S["ot_lo"], 1)

            def part_lo(part):
                lo, hi = (k * P for k in CAT_PARTS[part])
                for t in range(2):
                    dve.wait_ge(S["ot_hi"], 2 * part + t + 1)
                    dve.tensor_tensor(ring_lo[t][:, lo:hi], res[:, t, lo:hi],
                                      ring_hi[t][:, lo:hi].bitcast(F32), ALU.subtract)\
                       .then_inc(S["ot_lo"], 1)

            def wo_lo(n):
                dve.wait_ge(S["wo_hi"], n + 1)
                k = K_ORDER[n]
                dve.tensor_tensor(a_lo[:, k, :], stage[:, n % 2, :], a_hi[:, k, :].bitcast(F32),
                                  ALU.subtract).then_inc(S["wo_lo"], 1)

            while pool_at[0] < PG - 1 or pool_at[1] == 0:
                pool_op(NG)
            wo_lo(0)
            part_lo(0)
            pool_op(NG)
            wo_lo(1)
            wo_lo(2)
            norm_o(HEADS - 1)
            wo_lo(3)
            part_lo(1)
            wo_lo(4)
            part_lo(2)
            for n in range(5, KT):
                wo_lo(n)
            dve.wait_ge(S["norm_row_in"], 32)
            for t in range(TT):
                dve.wait_ge(x_in[t], 32)
                for n in range(2):
                    dve.wait_ge(S["res_mm"], 2 * t + n + 1)
                    c = slice(n * BANK, (n + 1) * BANK)
                    dve.tensor_tensor(res[:, t, c], res[:, t, c], bank(out_bank(t, n)), ALU.add)\
                       .then_inc(S["res_add"], 1)
                if t + 2 < TT:
                    ot_lo(t + 2)
                if t == TT - 1:
                    norm(TT + t, t)
                if t:
                    h_lo(TT + t - 1, t - 1, h2_hi, h2_lo, h2_bank(t - 1))
                if t < TT - 1:
                    norm(TT + t, t)
            h_lo(2 * TT - 1, TT - 1, h2_hi, h2_lo, h2_bank(TT - 1))

            def conv_up_op(n, e, gate_col, value_col, steps, evacs, tiles, lo_at):
                if n == 6:
                    dve.wait_ge(S["up_conv_step"], steps + 6)
                    dve.wait_ge(S["gate_silu"], tiles + 1)
                    dve.tensor_tensor(up_conv[:, e, 0, :], up_conv[:, e, 0, :], up_conv[:, e, 1, :],
                                      ALU.mult).then_inc(S["act_done"], 1)
                    return
                gu, tap = divmod(n, 3)
                col = (gate_col, value_col)[gu]
                y, z = up_conv[:, e, gu, :], up_raw[:, e, gu, :]
                if tap == 0:
                    dve.wait_ge(S["raw_evac"], evacs[gu])
                    if gu == 0 and lo_at is not None:
                        dve.wait_ge(S["act_lo_done"], lo_at)
                    dve.tensor_scalar(y, z, cols[:, 2, col], cols[:, 3, col], ALU.mult, ALU.add)\
                       .then_inc(S["up_conv_step"], 1)
                else:
                    dve.wait_ge(S["up_conv_step"], steps + n)
                    dve.scalar_tensor_tensor(y[:, tap:SEQ], z[:, 0:SEQ - tap], cols[:, 2 - tap, col],
                                             y[:, tap:SEQ], ALU.mult, ALU.add)\
                       .then_inc(S["up_conv_step"], 1)

            def add_down(downs, idx):
                t, n = divmod(idx, 2)
                dve.wait_ge(S["res_mm"], downs + (idx + 1))
                c = slice(n * BANK, (n + 1) * BANK)
                dve.tensor_tensor(res[:, t, c], res[:, t, c], bank(4 + idx % 4), ALU.add)\
                   .then_inc(S["res_add"], 1)

            for e in range(2):
                for n in range(7):
                    conv_up_op(n, e, slice(e, e + 1), slice(FT + e, FT + e + 1), 6 * e,
                               ((3, 4), (6, 8))[e], e, None)
            with dve.Fori(0, (FG - 1) // 2) as m:
                for b in range(2):
                    def tile_op(n, e):
                        tile = 2 * (b + 1) + e
                        conv_up_op(n, e, bass.ds(m * 4 + tile, 1), bass.ds(m * 4 + (FT + tile), 1),
                                   m * 24 + 6 * tile,
                                   (m * 16 + (4 * tile + 2), m * 16 + (4 * tile + 4)), m * 4 + tile,
                                   m * 4 + (tile - 1))

                    for n in range(7):
                        tile_op(n, 0)
                    for n in range(3):
                        tile_op(n, 1)
                    dve.wait_ge(S["res_add"], m * 32 + 16 * (b + 1))
                    for idx in range(16):
                        add_down(m * 32 + 16 * (b + 1), idx)
                        if idx % 2 == 0 and idx < 8:
                            tile_op(3 + idx // 2, 1)
            dve.wait_ge(S["res_add"], 16 * FG)

            def final(t):
                dve.wait_ge(S["final_r"], t + 1)
                dve.scalar_tensor_tensor(res[:, t, :], res[:, t, :], stats[:, 2, t:t + 1],
                                         norm_row[:, :], ALU.mult, ALU.mult)\
                   .then_inc(S["final_done"], 1)

            dve.wait_ge(S["norm_row_in"], 48)
            for t in range(TT):
                add_down(16 * FG, 2 * t)
                add_down(16 * FG, 2 * t + 1)
                if t:
                    final(t - 1)
            final(TT - 1)

        @block.tensor
        def _(pe):
            def transpose_tile(n, b):
                pe.wait_ge(S["normed_done"], n + 1)
                if n >= 2:
                    pe.wait_ge(S["h_lo"], n - 1)
                for k in range(KT):
                    last = pe.matmul(bank(b, 2)[:, k * P:(k + 1) * P], normed[:, n % 2, k * P:(k + 1) * P],
                                     ident[:, :], start=True, stop=True, is_transpose=True)
                last.then_inc(S["normed_T"], 1)

            def three(out_, l_hi, l_lo, r_hi, r_lo, first, final):
                pe.matmul(out_, l_hi, r_hi, start=first, stop=False)
                pe.matmul(out_, l_lo, r_hi, start=False, stop=False)
                return pe.matmul(out_, l_hi, r_lo, start=False, stop=final)

            at = [0, 0]

            def dense(n, only_pass=HEADS, until=NG):
                for _ in range(n):
                    g, u = at
                    if g >= until or GROUPS[g][1] > only_pass:
                        return
                    kind, i, j, half = GROUPS[g]
                    c = slice(half * HALF, (half + 1) * HALF)
                    if u == 0:
                        if g >= 2:
                            pe.wait_ge(S["dense_evac"], g - 1)
                        if kind == "proj":
                            pe.wait_ge(S["slab_lo"], 4 * i + j + 1)
                            if i == 0:
                                pe.wait_ge(S["h_lo"], 4 * (half + 1))
                        else:
                            pe.wait_ge(S["pool_w_in"], 16)
                            pe.wait_ge(S["pooled_step"], sum(2 * (PG - a) + 2 for a in range(j + 1)))
                    if kind == "lin":
                        last = pe.matmul(bank(g % 2), pool_wt[:, PG - 1 - j, :], raw[:, j % 2, c],
                                         start=True, stop=True)
                    else:
                        k, part = divmod(u, 3)
                        slot, ks = (4 * i + j) % 2, slice(k * P, (k + 1) * P)
                        w, a = ((ring_hi, a_hi), (ring_lo, a_hi), (ring_hi, a_lo))[part]
                        last = pe.matmul(bank(g % 2), w[slot][:, ks], a[:, k, c], start=(u == 0),
                                         stop=(u == UNITS[g] - 1))
                    at[1] += 1
                    if at[1] == UNITS[g]:
                        last.then_inc(S["dense_done"], 1)
                        at[:] = [g + 1, 0]

            def chunks(out_cols, l_of, r_of, done, banked):
                for b in range(TT):
                    for par in range(2):
                        last = pe.matmul(banked[rows_of(par), b * out_cols:(b + 1) * out_cols],
                                         l_of(par, b), r_of(par, b), start=True, stop=True)
                last.then_inc(S[done], 1)

            def blk64(ap):
                return lambda par, b: ap[rows_of(par), b * CHUNK:(b + 1) * CHUNK]

            def tok64(ap):
                return lambda par, b: ap[:, b * P + par * CHUNK:b * P + (par + 1) * CHUNK]

            def sum_of_squares(b, src, done):
                for half in range(2):
                    last = pe.matmul(bank(b + half), ones[:, :], src[:, half * HALF:(half + 1) * HALF],
                                     start=True, stop=True)
                last.then_inc(S[done], 1)

            def norm_o(h):
                pe.wait_ge(S["sqo_done"], h + 1)
                pe.wait_ge(S["s_upd"], (NCH + 1) * (h + 1))
                sum_of_squares(6, v_tok, "sumsq_o_mm")

            def gates(half):
                pe.wait_ge(S["h_lo"], 4 * (half + 1))
                c = slice(half * HALF, (half + 1) * HALF)
                for k in range(KT):
                    last = three(bank(6 + half)[0:8, :], wba_hi[:, k, :], wba_lo[:, k, :],
                                 a_hi[:, k, c], a_lo[:, k, c], k == 0, k == KT - 1)
                last.then_inc(S["ba_mm"], 1)

            pe.wait_ge(S["ident_done"], 2)
            for t in range(4):
                transpose_tile(t, 2 + 2 * (t % 2))
            pe.wait_ge(S["ba_w_split"], 2)
            gates(0)
            for t in range(4, TT):
                transpose_tile(t, 2 + 2 * (t % 2))
                dense(12, 0)
            gates(1)
            pe.wait_ge(S["rows_in"], 96)
            pe.wait_ge(S["ba_evac"], 1)
            for a in range(11):
                last = pe.matmul(bank(6)[:, 44 * a:44 * (a + 1)], rows[0:44, a, :], ident[0:44, 0:44],
                                 start=True, stop=True, is_transpose=True)
            last.then_inc(S["cols_T"], 1)
            dense(24, 0)
            pe.wait_ge(S["ba_evac"], 2)
            for t in range(TT):
                last = pe.matmul(bank(7)[:, 8 * t:8 * t + 8], ba_T[:, t * P:(t + 1) * P],
                                 ident[0:8, 0:8], start=True, stop=True, is_transpose=True)
            last.then_inc(S["ba_T_mm"], 1)
            dense(48, 0)
            pe.wait_ge(S["sc_dve"], 14)
            pe.wait_ge(S["cols_done"], 1)
            pe.wait_ge(S["consts_done"], 8)
            gs = g_tok[:, :, :].rearrange("p h b -> p (h b)")
            for n, m in enumerate((tri[:, :], suf[:, :], half_ones[:, 0, :], half_ones[:, 1, :])):
                last = pe.matmul(bank(6)[:, n * HEADS * TT:(n + 1) * HEADS * TT], m, gs, start=True,
                                 stop=True)
            last.then_inc(S["cum_mm"], 1)
            dense(10 ** 6, 0)
            for i in range(1, HEADS + 1):
                h = i - 1
                for step, filler in STEPS:
                    if step == "start":
                        pass
                    elif step == "norm_o":
                        if h:
                            norm_o(h - 1)
                    elif step == "sumsq_q":
                        pe.wait_ge(S["sumsq_in"], 2 * h + 1)
                        if h:
                            pe.wait_ge(S["o_evac"], 2 * h)
                        sum_of_squares(4, k_be, "sumsq_q_mm")
                    elif step == "vT":
                        if h:
                            pe.wait_ge(S["ln_o"], h)
                        pe.wait_ge(S["silu_done"], 3 * h + 3)
                        for b in range(TT):
                            last = pe.matmul(bank(6, 2)[:, b * P:(b + 1) * P], qkv[:, 2, b * P:(b + 1) * P],
                                             ident[:, :], start=True, stop=True, is_transpose=True)
                        last.then_inc(S["v_T_mm"], 1)
                    elif step == "sumsq_k":
                        pe.wait_ge(S["sumsq_in"], 2 * h + 2)
                        sum_of_squares(2, gam_flat, "sumsq_k_mm")
                    elif step == "decay":
                        pe.wait_ge(S["rhs_done"], 3 * h + 2)
                        pe.wait_ge(S["lnq"], h + 1)
                        pe.matmul(bank(4), tri[:, :], r1, start=True, stop=True)
                        pe.matmul(bank(5), suf[:, :], r2, start=True, stop=True)\
                          .then_inc(S["decay_mm"], 1)
                    elif step == "decay_row":
                        pe.wait_ge(S["lnk"], h + 1)
                        pe.matmul(bank(2), half_ones[:, 0, :], r2, start=True, stop=True)
                        pe.matmul(bank(3), half_ones[:, 1, :], r2, start=True, stop=True)\
                          .then_inc(S["decay_row_mm"], 1)
                    elif step == "beta_kk":
                        pe.wait_ge(S["gam_done"], h + 1)
                        pe.wait_ge(S["rhs_done"], 3 * h + 3)
                        pe.matmul(bank(4), blk_ones[:, :], r3, start=True, stop=True)\
                          .then_inc(S["beta_mm"], 1)
                        pe.wait_ge(S["kn_done"], h + 1)
                        chunks(CHUNK, tok64(qkv[:, 1, :]), tok64(qkv[:, 1, :]), "kk_mm", bank(5))
                    elif step == "qk":
                        pe.wait_ge(S["erow_done"], h + 1)
                        pe.wait_ge(S["qn_done"], h + 1)
                        chunks(CHUNK, tok64(qkv[:, 1, :]), tok64(qkv[:, 0, :]), "qk_mm", bank(2))
                    elif step == "kT":
                        pe.wait_ge(S["l1_done"], h + 1)
                        for b in range(TT):
                            last = pe.matmul(bank(4, 2)[:, b * P:(b + 1) * P], qkv[:, 1, b * P:(b + 1) * P],
                                             ident[:, :], start=True, stop=True, is_transpose=True)
                        last.then_inc(S["k_T_mm"], 1)
                    elif step.startswith("level") and step.endswith("a"):
                        lv = int(step[5])
                        pe.wait_ge(S["bt_done"], LEVELS * h + lv + 1)
                        pe.wait_ge(S["x_upd"], LEVELS * h + lv + 1)
                        if lv == 0:
                            pe.wait_ge(S["aqk_done"], 2 * (h + 1))
                        chunks(CHUNK, blk64(bt[lv % 2]), blk64(xinv), "t1_mm", bank(2))
                    elif step.startswith("level"):
                        lv = int(step[5])
                        pe.wait_ge(S["t1_evac"], LEVELS * h + lv + 1)
                        pe.wait_ge(S["xt_upd"], (LEVELS + 1) * h + lv + 1)
                        if lv == 0:
                            pe.wait_ge(S["kd_done"], h + 1)
                        if lv < LEVELS - 1:
                            chunks(CHUNK, blk64(xinvT), blk64(t1), "x_mm", bank(3))
                        chunks(CHUNK, blk64(t1), blk64(xinvT), "xt_mm", bank(4))
                    elif step == "u":
                        pe.wait_ge(S["xt_upd"], (LEVELS + 1) * (h + 1))
                        pe.wait_ge(S["vb_done"], h + 1)
                        chunks(P, blk64(xinvT), lambda par, b: v_tok[rows_of(par), b * P:(b + 1) * P],
                               "u_mm", bank(2, 2))
                    elif step == "w":
                        for b in range(TT):
                            for par in range(2):
                                last = pe.matmul(bank(4 + par)[:, b * CHUNK:(b + 1) * CHUNK],
                                                 k_be[rows_of(par), b * P:(b + 1) * P],
                                                 blk64(xinvT)(par, b), start=True, stop=True)
                        last.then_inc(S["w_mm"], 1)
                    elif step.endswith("a"):
                        c = int(step[5:-1])
                        par, b = c % 2, c // 2
                        if c == 0:
                            pe.wait_ge(S["w_evac"], h + 1)
                        if c == 0 and h:
                            pe.wait_ge(S["o_evac"], 2 * h)
                        pe.wait_ge(S["s_upd"], (NCH + 1) * h + c + 1)
                        pe.matmul(bank(6)[rows_of(par), 0:P],
                                  wT[:, par * HALF + b * CHUNK:][:, 0:CHUNK], state, start=True,
                                  stop=True).then_inc(S["v_mm"], 1)
                        o_at = bank(o_bank(c))[:, (c % 8) * CHUNK:(c % 8 + 1) * CHUNK]
                        pe.matmul(o_at, state, tok64(qg)(par, b), start=(par == 0), stop=False)
                    else:
                        c = int(step[5:-1])
                        par, b = c % 2, c // 2
                        r = rows_of(par)
                        pe.wait_ge(S["v_new_done"], NCH * h + c + 1)
                        pe.matmul(bank(6)[:, P:2 * P], k_d[r, b * P:(b + 1) * P], v_new[r, :],
                                  start=True, stop=True).then_inc(S["s_mm"], 1)
                        if par:
                            o_at = bank(o_bank(c))[:, (b % 4) * P:(b % 4 + 1) * P]
                            last = pe.matmul(o_at, v_new, aqkT[:, b, :, :].rearrange("p a n -> p (a n)"),
                                             start=False, stop=True)
                        if c % 8 == 7:
                            last.then_inc(S["o_mm"], 1)
                    dense(filler, i)
                if i < HEADS:
                    dense(10 ** 6, i)
            dense(10 ** 6, HEADS, INDEX[("lin", HEADS, 2, 1)] + 1)
            norm_o(HEADS - 1)

            def out_product(t, n, k):
                ks, c = slice(k * P, (k + 1) * P), slice(n * BANK, (n + 1) * BANK)
                return three(bank(out_bank(t, n)), ring_hi[t % 2][:, ks], ring_lo[t % 2][:, ks],
                             a_hi[:, k, c], a_lo[:, k, c], k == K_ORDER[0], k == K_ORDER[-1])

            BOTH = KT - 2
            for i, k in enumerate(K_ORDER[:BOTH]):
                pe.wait_ge(S["wo_lo"], i + 1)
                pe.wait_ge(S["ot_lo"], 2 * part_of(k) + 2)
                for t in range(2):
                    for n in range(2):
                        out_product(t, n, k)
                if i == 0:
                    dense(10 ** 6, HEADS)
            for t in range(2):
                for i, k in enumerate(K_ORDER[BOTH:]):
                    pe.wait_ge(S["wo_lo"], BOTH + i + 1)
                    pe.wait_ge(S["ot_lo"], 2 * part_of(k) + t + 1)
                    for n in range(2):
                        last = out_product(t, n, k)
                        if k == K_ORDER[-1]:
                            last.then_inc(S["res_mm"], 1)
            for t in range(2, TT):
                pe.wait_ge(S["ot_lo"], tile_split(t))
                if t == 2:
                    pe.wait_ge(S["dense_evac"], NG)
                else:
                    pe.wait_ge(S["res_add"], 2 if t == 3 else 2 * (t - 1))
                for n in range(2):
                    for k in K_ORDER:
                        last = out_product(t, n, k)
                    last.then_inc(S["res_mm"], 1)
                    if t == 2 and n == 0:
                        transpose_tile(TT, h2_bank(0))
                transpose_tile(TT + t - 1, h2_bank(t - 1))

            def up_half(ring, gu, half):
                c = slice(half * HALF, (half + 1) * HALF)
                for k in range(KT):
                    ks = slice(k * P, (k + 1) * P)
                    last = three(bank(2 * gu + half), ring_hi[ring][:, ks], ring_lo[ring][:, ks],
                                 h2_hi[:, k, c], h2_lo[:, k, c], k == 0, k == KT - 1)
                last.then_inc(S["up_mm"], 1)

            def up(slabs, evacs, ring_at):
                for n in range(4):
                    pe.wait_ge(S["ffn_lo"], slabs + (n + 1))
                    for half in range(2):
                        pe.wait_ge(S["raw_evac"], evacs + (2 * n + half - 3))
                        up_half((ring_at + n) % 3, n % 2, half)

            def down(slabs, acts, adds, par, rings):
                pe.wait_ge(S["ffn_lo"], slabs)
                pe.wait_ge(S["act_lo_done"], acts)
                for idx in range(16):
                    t, n = divmod(idx, 2)
                    pe.wait_ge(S["res_add"], adds + (idx + 13))
                    ts_, c = slice(t * P, (t + 1) * P), slice(n * BANK, (n + 1) * BANK)
                    for e in range(2):
                        ring = rings[e]
                        last = three(bank(4 + idx % 4), act_hi[:, 2 * par + e, ts_],
                                     act_lo[:, 2 * par + e, ts_], ring_hi[ring][:, c],
                                     ring_lo[ring][:, c], e == 0, e == 1)
                    last.then_inc(S["res_mm"], 1)

            for gu, half in ((0, 0), (1, 0), (0, 1), (1, 1)):
                pe.wait_ge(S["ffn_lo"], gu + 1)
                pe.wait_ge(S["h_lo"], TT + 4 * (half + 1))
                pe.wait_ge(S["res_add"], 2 * (TT - 1 + gu))
                up_half(gu, gu, half)
                if gu == half == 0:
                    transpose_tile(2 * TT - 1, h2_bank(TT - 1))
            for n, evacs in ((2, (1, 3)), (3, (3, 4))):
                pe.wait_ge(S["ffn_lo"], n + 1)
                for half in range(2):
                    pe.wait_ge(S["raw_evac"], evacs[half])
                    up_half(n % 3, n % 2, half)
            with pe.Fori(0, (FG - 1) // 2) as m:
                for b in range(2):
                    up(m * 12 + (4 + 6 * b), m * 16 + 8 * (1 + b), 1)
                    down(m * 12 + (10 + 6 * b), m * 4 + (2 + 2 * b), m * 32 + 16 * b, b, (2, 0))
            down(4 + 6 * (FG - 1) + 2, 2 * FG, 16 * (FG - 1), (FG - 1) % 2, (1, SPARE))


_INS = ["x", "norm1_w", "w_in", "conv_qkv_w", "a_log", "dt_bias", "onorm_w", "pool_w", "pool_b",
        "pool_scale", "w_out", "norm2_w", "w_up", "ffn_conv_w", "ffn_conv_b", "w_down",
        "final_norm_w"]


def kernel(**inputs):
    import concourse.bacc as bacc
    from concourse.bass_utils import run_bass_kernel_spmd

    nc = bacc.Bacc("TRN2", target_bir_lowering=False, num_devices=1,
                   dynamic_dma_scratch_size=1024)
    arrays, args = {}, []
    for name in _INS:
        a = np.ascontiguousarray(inputs[name])
        arrays[f"in_{name}"] = a
        args.append(nc.dram_tensor(f"in_{name}", a.shape, mybir.dt.from_np(a.dtype),
                                   kind="ExternalInput").ap())
    out = nc.dram_tensor("out_y", inputs["x"].shape, F32, kind="ExternalOutput").ap()
    block_program(nc, *args, out)
    r = run_bass_kernel_spmd(nc, [arrays], core_ids=[0])
    return r.results[0]["out_y"]
```
